# Optimizing a Trainium2 kernel written in Bass

```python
import jax, jax.numpy as jnp
from jax import lax
import numpy as np

D_MODEL = 1024
BATCH = 1
SEQ = 1024
DEPTH = 1

GRID_W = 64
CTX_LEN = 256
NA_HEADS = 8
NA_HEAD_DIM = 64
NA_WIDTH = NA_HEADS * NA_HEAD_DIM
NA_WIN_ROWS = 8
NA_WIN_COLS = 16
LRU_WIDTH = D_MODEL
LRU_BLOCKS = 8
LRU_BLOCK = LRU_WIDTH // LRU_BLOCKS
CONV_WIDTH = 4
CONV_LEFT = 2
LRU_C = 8.0
PEER_HEADS = 8
PEER_NKEYS = 128
PEER_EXPERTS = PEER_NKEYS * PEER_NKEYS
PEER_QDIM = 256
PEER_HALF = PEER_QDIM // 2
PEER_TOPK = 16
PEER_CHUNK = 128
EPS = 1e-6
NEG_INF = -1e30

Q0 = 0
K0 = Q0 + NA_WIDTH
V0 = K0 + NA_WIDTH
XR0 = V0 + NA_WIDTH
YR0 = XR0 + LRU_WIDTH
GA0 = YR0 + LRU_WIDTH
GB0 = GA0 + D_MODEL
IN_COLS = GB0 + D_MODEL

kernel_name = "hybrid_na_rglru_peer_dit_block"

def rms_norm(x, w):
    xf = x.astype(jnp.float32)
    y = xf * lax.rsqrt(jnp.mean(xf * xf, axis=-1, keepdims=True) + EPS)
    return (y * w.astype(jnp.float32)).astype(x.dtype)

def modulate(h, shift, scale):
    return h * (1.0 + scale[:, None, :]) + shift[:, None, :]

def dwconv_centred(u, w, b):
    T = u.shape[1]
    up = jnp.pad(u, ((0, 0), (CONV_LEFT, CONV_WIDTH - 1 - CONV_LEFT), (0, 0)))
    out = b
    for j in range(CONV_WIDTH):
        out = out + w[j] * up[:, j:j + T]
    return out

def rglru_coeffs(u, w_a, b_a, w_x, b_x, lam):
    B, T, W = u.shape
    uf = u.astype(jnp.float32)
    ub = uf.reshape(B, T, LRU_BLOCKS, LRU_BLOCK)
    r = jax.nn.sigmoid(jnp.einsum('btnc,ncd->btnd', ub, w_a.astype(jnp.float32)).reshape(B, T, W) + b_a)
    i = jax.nn.sigmoid(jnp.einsum('btnc,ncd->btnd', ub, w_x.astype(jnp.float32)).reshape(B, T, W) + b_x)
    log_a = -LRU_C * r * jax.nn.softplus(-lam.astype(jnp.float32))
    a = jnp.exp(log_a)
    beta = jnp.sqrt(-jnp.expm1(2.0 * log_a))
    return a, beta * (i * uf)

def linear_scan(a, b, reverse):
    def combine(left, right):
        a_l, b_l = left
        a_r, b_r = right
        return a_l * a_r, a_r * b_l + b_r
    _, h = lax.associative_scan(combine, (a, b), reverse=reverse, axis=1)
    return h

def rglru_bidirectional(u_lat, u_ctx, w_a, b_a, w_x, b_x, lam):
    out = None
    for d, rev in enumerate((False, True)):
        a_c, b_c = rglru_coeffs(u_ctx, w_a[d], b_a[d], w_x[d], b_x[d], lam[d])
        h_c = linear_scan(a_c, b_c, rev)
        a_l, b_l = rglru_coeffs(u_lat, w_a[d], b_a[d], w_x[d], b_x[d], lam[d])
        if rev:
            b_l = b_l.at[:, -1].add(a_l[:, -1] * h_c[:, 0])
        else:
            b_l = b_l.at[:, 0].add(a_l[:, 0] * h_c[:, -1])
        h_l = linear_scan(a_l, b_l, rev)
        out = h_l if out is None else out + h_l
    return out

def neighbourhood_attention(q, k, v, k_ctx, v_ctx, rpb):
    B, S = q.shape[0], q.shape[1]
    rows = S // GRID_W
    wr = min(NA_WIN_ROWS, rows)
    wc = NA_WIN_COLS
    grid = lambda t: t.reshape(B, rows, GRID_W, NA_HEADS, NA_HEAD_DIM)
    qg, kg, vg = grid(q), grid(k), grid(v)
    r = jnp.arange(rows)
    row0 = jnp.clip(r - wr // 2, 0, rows - wr)
    key_rows = row0[:, None] + jnp.arange(wr)
    k_strip = kg[:, key_rows]
    v_strip = vg[:, key_rows]
    col = jnp.arange(GRID_W)
    col0 = jnp.clip(col - wc // 2, 0, GRID_W - wc)
    col_mask = (col[None, :] >= col0[:, None]) & (col[None, :] < col0[:, None] + wc)
    dr = key_rows - r[:, None]
    dc = jnp.clip(col[None, :] - col[:, None], -(wc - 1), wc - 1)
    bias = rpb[:, dr[:, None, :, None] + NA_WIN_ROWS - 1,
               dc[None, :, None, :] + NA_WIN_COLS - 1]
    scale = NA_HEAD_DIM ** -0.5
    s_win = jnp.einsum('brqhd,brwkhd->bhrqwk', qg, k_strip).astype(jnp.float32) * scale
    s_win = jnp.where(col_mask[:, None, :], s_win + bias.astype(jnp.float32), NEG_INF)
    s_ctx = jnp.einsum('brqhd,bchd->bhrqc', qg, k_ctx).astype(jnp.float32) * scale
    n_win = wr * GRID_W
    s = jnp.concatenate([s_win.reshape(B, NA_HEADS, rows, GRID_W, n_win), s_ctx], axis=-1)
    p = jax.nn.softmax(s, axis=-1).astype(v.dtype)
    p_win = p[..., :n_win].reshape(B, NA_HEADS, rows, GRID_W, wr, GRID_W)
    p_ctx = p[..., n_win:]
    o = (jnp.einsum('bhrqwk,brwkhd->brqhd', p_win, v_strip)
         + jnp.einsum('bhrqc,bchd->brqhd', p_ctx, v_ctx))
    return o.reshape(B, S, NA_WIDTH)

def peer(h, w_q, keys, u, v):
    B, S, D = h.shape
    q = (h @ w_q).reshape(B, S, PEER_HEADS, 2, PEER_HALF)
    s = jnp.einsum('bshpd,hpkd->bshpk', q, keys).astype(jnp.float32)
    top_s, top_i = lax.top_k(s, PEER_TOPK)
    cand_s = (top_s[..., 0, :, None] + top_s[..., 1, None, :]).reshape(B, S, PEER_HEADS, PEER_TOPK * PEER_TOPK)
    cand_i = (top_i[..., 0, :, None] * PEER_NKEYS + top_i[..., 1, None, :]).reshape(B, S, PEER_HEADS, PEER_TOPK * PEER_TOPK)
    best_s, pos = lax.top_k(cand_s, PEER_TOPK)
    expert = jnp.take_along_axis(cand_i, pos, axis=-1)
    gate = jax.nn.softmax(best_s, axis=-1).astype(h.dtype)
    n_chunks = (B * S) // PEER_CHUNK

    def chunk(args):
        hc, ec, gc = args
        act = jax.nn.gelu(jnp.einsum('td,thkd->thk', hc, u[ec]))
        return jnp.einsum('thk,thkd->td', gc * act, v[ec])

    y = lax.map(chunk, (h.reshape(n_chunks, PEER_CHUNK, D),
                        expert.reshape(n_chunks, PEER_CHUNK, PEER_HEADS, PEER_TOPK),
                        gate.reshape(n_chunks, PEER_CHUNK, PEER_HEADS, PEER_TOPK)))
    return y.reshape(B, S, D)

def setup_inputs(seed: int = 0) -> dict:
    key = jax.random.key(seed)
    ks = jax.random.split(key, 26)
    nrm = lambda k, shape, s: jax.random.normal(k, shape, jnp.float32) * s
    a0 = jax.random.uniform(ks[18], (DEPTH, 2, LRU_WIDTH), jnp.float32, 0.9, 0.999)
    p0 = a0 ** (1.0 / LRU_C)
    return {
        "x": nrm(ks[0], (BATCH, SEQ, D_MODEL), 1.0),
        "c": nrm(ks[1], (BATCH, D_MODEL), 1.0),
        "ctx": nrm(ks[2], (BATCH, CTX_LEN, D_MODEL), 1.0),
        "c_ctx": nrm(ks[3], (D_MODEL,), 1.0),
        "w_ada": nrm(ks[4], (DEPTH, D_MODEL, 6 * D_MODEL), 0.5 * D_MODEL ** -0.5),
        "b_ada": nrm(ks[5], (DEPTH, 6 * D_MODEL), 0.02),
        "norm1_w": 1.0 + nrm(ks[6], (DEPTH, D_MODEL), 0.02),
        "norm2_w": 1.0 + nrm(ks[7], (DEPTH, D_MODEL), 0.02),
        "w_in": nrm(ks[8], (DEPTH, D_MODEL, IN_COLS), D_MODEL ** -0.5),
        "q_norm_w": 1.0 + nrm(ks[9], (DEPTH, NA_HEAD_DIM), 0.02),
        "k_norm_w": 1.0 + nrm(ks[10], (DEPTH, NA_HEAD_DIM), 0.02),
        "na_rpb": nrm(ks[11], (DEPTH, NA_HEADS, 2 * NA_WIN_ROWS - 1, 2 * NA_WIN_COLS - 1), 0.1),
        "conv_w": nrm(ks[12], (DEPTH, CONV_WIDTH, LRU_WIDTH), CONV_WIDTH ** -0.5),
        "conv_b": nrm(ks[13], (DEPTH, LRU_WIDTH), 0.02),
        "lru_w_a": nrm(ks[14], (DEPTH, 2, LRU_BLOCKS, LRU_BLOCK, LRU_BLOCK), LRU_BLOCK ** -0.5),
        "lru_b_a": nrm(ks[15], (DEPTH, 2, LRU_WIDTH), 0.02),
        "lru_w_x": nrm(ks[16], (DEPTH, 2, LRU_BLOCKS, LRU_BLOCK, LRU_BLOCK), LRU_BLOCK ** -0.5),
        "lru_b_x": nrm(ks[17], (DEPTH, 2, LRU_WIDTH), 0.02),
        "lru_lambda": jnp.log(p0) - jnp.log1p(-p0),
        "w_o_attn": nrm(ks[19], (DEPTH, NA_WIDTH, D_MODEL), NA_WIDTH ** -0.5),
        "w_o_lru": nrm(ks[20], (DEPTH, LRU_WIDTH, D_MODEL), LRU_WIDTH ** -0.5),
        "w_out": nrm(ks[21], (DEPTH, D_MODEL, D_MODEL), D_MODEL ** -0.5),
        "peer_w_q": nrm(ks[22], (DEPTH, D_MODEL, PEER_HEADS * PEER_QDIM), D_MODEL ** -0.5),
        "peer_keys": nrm(ks[23], (DEPTH, PEER_HEADS, 2, PEER_NKEYS, PEER_HALF), PEER_HALF ** -0.5),
        "peer_u": nrm(ks[24], (DEPTH, PEER_EXPERTS, D_MODEL), D_MODEL ** -0.5),
        "peer_v": nrm(ks[25], (DEPTH, PEER_EXPERTS, D_MODEL), PEER_HEADS ** -0.5),
    }

def reference(x, c, ctx, c_ctx, w_ada, b_ada, norm1_w, norm2_w, w_in, q_norm_w, k_norm_w, na_rpb,
              conv_w, conv_b, lru_w_a, lru_b_a, lru_w_x, lru_b_x, lru_lambda, w_o_attn, w_o_lru,
              w_out, peer_w_q, peer_keys, peer_u, peer_v):
    B, S, D = x.shape
    C = ctx.shape[1]
    for layer in range(DEPTH):
        mod = jax.nn.silu(c) @ w_ada[layer] + b_ada[layer]
        shift1, scale1, gate1, shift2, scale2, gate2 = jnp.split(mod, 6, axis=-1)
        mod_c = jax.nn.silu(c_ctx) @ w_ada[layer] + b_ada[layer]
        shift1_c, scale1_c = mod_c[:D], mod_c[D:2 * D]

        h = modulate(rms_norm(x, norm1_w[layer]), shift1, scale1)
        z = h @ w_in[layer]
        hc = rms_norm(ctx, norm1_w[layer]) * (1.0 + scale1_c) + shift1_c
        zc = hc @ w_in[layer][:, K0:YR0]

        q = rms_norm(z[..., Q0:K0].reshape(B, S, NA_HEADS, NA_HEAD_DIM), q_norm_w[layer])
        k = rms_norm(z[..., K0:V0].reshape(B, S, NA_HEADS, NA_HEAD_DIM), k_norm_w[layer])
        v = z[..., V0:XR0].reshape(B, S, NA_HEADS, NA_HEAD_DIM)
        k_c = rms_norm(zc[..., :NA_WIDTH].reshape(B, C, NA_HEADS, NA_HEAD_DIM), k_norm_w[layer])
        v_c = zc[..., NA_WIDTH:2 * NA_WIDTH].reshape(B, C, NA_HEADS, NA_HEAD_DIM)
        o_a = neighbourhood_attention(q, k, v, k_c, v_c, na_rpb[layer])

        u = dwconv_centred(z[..., XR0:YR0], conv_w[layer], conv_b[layer])
        u_c = dwconv_centred(zc[..., 2 * NA_WIDTH:], conv_w[layer], conv_b[layer])
        h_r = rglru_bidirectional(u, u_c, lru_w_a[layer], lru_b_a[layer], lru_w_x[layer],
                                  lru_b_x[layer], lru_lambda[layer])
        o_b = h_r.astype(x.dtype) * jax.nn.gelu(z[..., YR0:GA0])

        merged = (jax.nn.sigmoid(z[..., GA0:GB0]) * (o_a @ w_o_attn[layer])
                  + jax.nn.sigmoid(z[..., GB0:]) * (o_b @ w_o_lru[layer]))
        x = x + gate1[:, None, :] * (merged @ w_out[layer])

        h2 = modulate(rms_norm(x, norm2_w[layer]), shift2, scale2)
        y = peer(h2, peer_w_q[layer], peer_keys[layer], peer_u[layer], peer_v[layer])
        x = x + gate2[:, None, :] * y
    return x


_drawn_inputs = setup_inputs


def setup_inputs(seed=0):
    import zlib

    import numpy as np

    out = dict(_drawn_inputs(seed))
    spreads = {}
    factors = {'norm1_w': 5.991,
     'norm2_w': 36.161,
     'q_norm_w': 8.0,
     'k_norm_w': 8.0,
     'na_rpb': 39.034,
     'lru_b_a': 22.628,
     'lru_b_x': 8.0}
    for name, (base, spread) in spreads.items():
        noise = np.random.default_rng([zlib.crc32(name.encode()), seed]).standard_normal(out[name].shape)
        drawn = base * np.exp(spread * noise) if base else spread * noise
        out[name] = __import__('jax').numpy.asarray(drawn.astype(out[name].dtype))
    for name, factor in factors.items():
        out[name] = (out[name] * factor).astype(out[name].dtype)
    return out
```

```python
from contextlib import ExitStack

import numpy as np

import concourse.bass as bass
from concourse import mybir

F32 = mybir.dt.float32
F32R = mybir.dt.float32r
BF16 = mybir.dt.bfloat16
U32 = mybir.dt.uint32
ALU = mybir.AluOpType
ACT = mybir.ActivationFunctionType
AX_X = mybir.AxisListType.X

P = 128
D = 1024
KD = D // P
T = 1024
C = 256
TC = T + C
HALF = 512
EPS = 1e-6
NEG = -1e30

HEADS = 8
HD = 64
PAIRS = HEADS // 2
GRID_W = 64
ROWS = T // GRID_W
WIN = 8
WIN_COLS = 16
DR = 2 * WIN - 1
SCALE = HD ** -0.5
VT = TC // P
VS = T // P - 1

BLOCKS = 8
CONV = 4
CONV_LEFT = 2

NK = 128
TOPK = 16
PH = 8
TT = T // P
NEXP = NK * NK


def split_columns(n):
    return [(a, min(n, a + HALF)) for a in range(0, n, HALF)]


def product3(nc, out, w_hi, w_lo, x_hi, x_lo, first, last):
    nc.tensor.matmul(out, w_hi, x_hi, start=first, stop=False)
    nc.tensor.matmul(out, w_hi, x_lo, start=False, stop=False)
    return nc.tensor.matmul(out, w_lo, x_hi, start=False, stop=last)


class Columns:

    def __init__(self, lat, con):
        self.lat, self.con = lat, con

    def at(self, k, a, b):
        return self.lat[:, k, a:b] if b <= T else self.con[:, k, a - T:b - T]


class Pool:

    def __init__(self, nc, ctx, prefix):
        self.nc, self.ctx, self.prefix = nc, ctx, prefix

    def sb(self, name, shape, dt=F32):
        return self.ctx.enter_context(self.nc.sbuf_tensor(f"{self.prefix}_{name}", shape, dt))

    def ps(self, name, shape):
        return self.ctx.enter_context(self.nc.psum_tensor(f"{self.prefix}_{name}", shape, F32))

    def sem(self, name):
        return self.ctx.enter_context(self.nc.semaphore(f"{self.prefix}_{name}"))


def adaln_and_norm1(nc, io, keep):
    PIECE = 512
    PIECES = 6 * D // PIECE
    GROUPS = PIECE // P
    with ExitStack() as ctx:
        m = Pool(nc, ctx, "a")
        xt = m.sb("xt", [P, KD, TC])
        w = m.sb("w", [P, 2, KD, PIECE])
        cc = m.sb("cc", [P, KD, 2])
        silu_c = m.sb("silu_c", [P, KD, 2])
        b_ada = m.sb("b_ada", [P, 6 * KD])
        ones = m.sb("ones", [P, P])
        eps = m.sb("eps", [P, 1])
        sq = m.sb("sq", [P, 2, TC])
        root = m.sb("root", [P, TC])
        rstd = m.sb("rstd", [P, TC])
        p1 = m.sb("p1", [P, 3, KD])
        hn = m.sb("hn", [P, 2, TC])
        hm = m.sb("hm", [P, 2, TC])
        ps_sum = m.ps("ps_sum", [P, 3 * HALF])
        ps_mod = m.ps("ps_mod", [P, HALF])
        x_in, small_in, out_done = m.sem("x_in"), m.sem("small_in"), m.sem("out_done")
        w_in = [m.sem(f"w_in{b}") for b in range(2)]
        w_used, silu_done, sq_done, sq_used = m.sem("w_used"), m.sem("silu_done"), m.sem("sq_done"), m.sem("sq_used")
        consts, root_done, mod_ready, vec = m.sem("consts"), m.sem("root_done"), m.sem("mod_ready"), m.sem("vec")
        normed, modulated, hi_done, lo_done = m.sem("normed"), m.sem("modulated"), m.sem("hi_done"), m.sem("lo_done")
        block = ctx.enter_context(nc.Block())

        @block.sync
        def _(sp):
            sp.dma_start(cc[:], io["cc"].rearrange("p (k v) -> p k v", v=2)).then_inc(small_in, 16)
            sp.dma_start(b_ada[:], io["b_ada"]).then_inc(small_in, 16)
            sp.dma_start(keep.norm_w[:], io["norm_w"]).then_inc(small_in, 16)
            sp.dma_start(xt[:, :, 0:T], io["xt"].rearrange("p (k t) -> p k t", k=KD)).then_inc(x_in, 16)
            sp.dma_start(xt[:, :, T:TC], io["ctxt"].rearrange("p (k t) -> p k t", k=KD)).then_inc(x_in, 16)
            with sp.Fori(0, PIECES // 2) as i:
                for b in range(2):
                    sp.wait_ge(w_used, 2 * i + b + 1)
                    sp.dma_start(w[:, b], io["w_ada"][2 * i + b].rearrange("p (k n) -> p k n", k=KD)).then_inc(w_in[b], 16)

        @block.scalar
        def _(act):
            act.wait_ge(small_in, 48)
            nc.scalar.activation(silu_c[:], cc[:], ACT.Silu).then_inc(silu_done, 1)
            act.wait_ge(x_in, 32)
            for k in range(KD):
                if k >= 2:
                    act.wait_ge(sq_used, k - 1)
                nc.scalar.activation(sq[:, k % 2], xt[:, k], ACT.Square).then_inc(sq_done, 1)
            act.wait_ge(sq_used, KD)
            act.wait_ge(consts, 2)
            nc.scalar.activation(root[:], ps_sum[:, 0:TC], ACT.Sqrt, bias=eps[:], scale=1.0 / D).then_inc(root_done, 1)
            for k in range(KD):
                act.wait_ge(modulated, 2 * k + 2)
                for a, b in ((0, T), (T, TC)):
                    nc.scalar.activation(keep.h_hi.at(k, a, b), hm[:, k % 2, a:b], ACT.Copy).then_inc(hi_done, 1)

        @block.tensor
        def _(pe):
            pe.wait_ge(consts, 2)
            for k in range(KD):
                pe.wait_ge(sq_done, k + 1)
                for a, b in split_columns(TC):
                    last = nc.tensor.matmul(ps_sum[:, a:b], ones[:], sq[:, k % 2, a:b], start=(k == 0), stop=(k == KD - 1))
                last.then_inc(sq_used, 1)
            pe.wait_ge(silu_done, 1)
            pe.sem_inc(w_used, 2)
            with pe.Fori(0, PIECES // 2) as i:
                for b in range(2):
                    pe.wait_ge(w_in[b], 16 * (i + 1))
                    for g in range(GROUPS):
                        col = (2 * i + b) * 2 * GROUPS + 2 * g
                        for k in range(KD):
                            last = nc.tensor.matmul(ps_mod[:, bass.ds(col, 2)], w[:, b, k, g * P:(g + 1) * P], silu_c[:, k, :],
                                                    start=(k == 0), stop=(k == KD - 1))
                    last.then_inc(w_used, 1)

        @block.vector
        def _(dve):
            nc.vector.memset(ones[:], 1.0).then_inc(consts, 1)
            nc.vector.memset(eps[:], EPS).then_inc(consts, 1)
            dve.wait_ge(root_done, 1)
            nc.vector.reciprocal(rstd[:], root[:]).then_inc(vec, 1)
            dve.wait_ge(w_used, 2 + PIECES)
            dve.wait_ge(small_in, 48)
            pm = ps_mod[:, 0:12 * KD].rearrange("p (n v) -> p n v", v=2)
            nc.vector.tensor_tensor(keep.mod[:], pm[:, :, 0], b_ada[:], ALU.add).then_inc(vec, 1)
            nc.vector.tensor_tensor(keep.mod_c[:], pm[:, 0:2 * KD, 1], b_ada[:, 0:2 * KD], ALU.add).then_inc(vec, 1)
            dve.wait_ge(vec, 3)
            nc.vector.tensor_scalar_add(p1[:, 0], keep.mod[:, KD:2 * KD], 1.0).then_inc(vec, 1)
            nc.vector.tensor_scalar_add(p1[:, 1], keep.mod_c[:, KD:2 * KD], 1.0).then_inc(vec, 1)
            nc.vector.tensor_scalar_add(p1[:, 2], keep.mod[:, 4 * KD:5 * KD], 1.0).then_inc(vec, 1)
            dve.wait_ge(vec, 6)
            nc.vector.tensor_tensor(keep.gain[:, 0], p1[:, 0], keep.norm_w[:, 0:KD], ALU.mult).then_inc(vec, 1)
            nc.vector.tensor_tensor(keep.gain[:, 1], p1[:, 1], keep.norm_w[:, 0:KD], ALU.mult).then_inc(vec, 1)
            nc.vector.tensor_tensor(keep.gain[:, 2], p1[:, 2], keep.norm_w[:, KD:2 * KD], ALU.mult).then_inc(vec, 1)
            dve.wait_ge(vec, 9)
            for k in range(KD):
                nc.vector.tensor_tensor(hn[:, k % 2], xt[:, k], rstd[:], ALU.mult).then_inc(normed, 1)
                dve.wait_ge(normed, k + 1)
                nc.vector.tensor_scalar(hm[:, k % 2, 0:T], hn[:, k % 2, 0:T], keep.gain[:, 0, k:k + 1], keep.mod[:, k:k + 1],
                                        ALU.mult, ALU.add).then_inc(modulated, 1)
                nc.vector.tensor_scalar(hm[:, k % 2, T:TC], hn[:, k % 2, T:TC], keep.gain[:, 1, k:k + 1], keep.mod_c[:, k:k + 1],
                                        ALU.mult, ALU.add).then_inc(modulated, 1)
                dve.wait_ge(hi_done, 2 * k + 2)
                for a, b in ((0, T), (T, TC)):
                    nc.vector.tensor_tensor(keep.h_lo.at(k, a, b), hm[:, k % 2, a:b], keep.h_hi.at(k, a, b).bitcast(F32), ALU.subtract)\
                        .then_inc(lo_done, 1)
                dve.wait_ge(lo_done, 2 * k + 2)


def values(nc, io, keep):
    W = HEADS * HD
    with ExitStack() as ctx:
        m = Pool(nc, ctx, "v")
        raw = m.sb("raw", [P, KD, W])
        w_hi = m.sb("w_hi", [P, KD, W], F32R)
        w_lo = m.sb("w_lo", [P, KD, W], F32R)
        v = m.sb("v", [P, 2, W])
        acc = m.ps("acc", [P, 2, W])
        w_in, hi_done, lo_done, acc_ready, v_ready = m.sem("w_in"), m.sem("hi_done"), m.sem("lo_done"), m.sem("acc_ready"), m.sem("v_ready")
        stored = [m.sem(f"stored{b}") for b in range(2)]
        block = ctx.enter_context(nc.Block())

        @block.sync
        def _(sp):
            sp.dma_start(raw[:], io["w_v"].rearrange("p (k n) -> p k n", k=KD)).then_inc(w_in, 16)
            for j in range(VT):
                sp.wait_ge(v_ready, j + 1)
                sp.dma_start(io["v_scr"][j * P:(j + 1) * P, :], v[:, j % 2]).then_inc(stored[j % 2], 16)
            for b in range(2):
                sp.wait_ge(stored[b], 16 * (VT // 2))

        @block.scalar
        def _(act):
            act.wait_ge(w_in, 16)
            for k in range(KD):
                nc.scalar.activation(w_hi[:, k], raw[:, k], ACT.Copy).then_inc(hi_done, 1)
            for j in range(VT):
                act.wait_ge(acc_ready, j + 1)
                if j >= 2:
                    act.wait_ge(stored[j % 2], 16 * (j // 2))
                nc.scalar.activation(v[:, j % 2], acc[:, j % 2], ACT.Copy).then_inc(v_ready, 1)

        @block.vector
        def _(dve):
            for k in range(KD):
                dve.wait_ge(hi_done, k + 1)
                nc.vector.tensor_tensor(w_lo[:, k], raw[:, k], w_hi[:, k].bitcast(F32), ALU.subtract).then_inc(lo_done, 1)

        @block.tensor
        def _(pe):
            for j in range(VT):
                if j >= 2:
                    pe.wait_ge(v_ready, j - 1)
                tile = (j * P, (j + 1) * P)
                for k in range(KD):
                    pe.wait_ge(lo_done, k + 1)
                    out = acc[:, j % 2]
                    nc.tensor.matmul(out, keep.h_hi.at(k, *tile), w_hi[:, k], start=(k == 0), stop=False)
                    nc.tensor.matmul(out, keep.h_hi.at(k, *tile), w_lo[:, k], start=False, stop=False)
                    last = nc.tensor.matmul(out, keep.h_lo.at(k, *tile), w_hi[:, k], start=False, stop=(k == KD - 1))
                last.then_inc(acc_ready, 1)


def attention(nc, io, keep):
    KEYS = WIN * GRID_W
    ALL = KEYS + C
    NT = ALL // P
    row0 = [min(max(r - WIN // 2, 0), ROWS - WIN) for r in range(ROWS)]
    with ExitStack() as ctx:
        m = Pool(nc, ctx, "at")
        raw = m.sb("raw", [P, 2, KD, P])
        w_hi = m.sb("w_hi", [P, 2, KD, P], F32R)
        w_lo = m.sb("w_lo", [P, 2, KD, P], F32R)
        qk_w = m.sb("qk_w", [P, 2])
        q_w = m.sb("q_w", [P, 1])
        head_ones = m.sb("head_ones", [P, P])
        ident = m.sb("ident", [P, P])
        eps = m.sb("eps", [P, 1])
        mask = m.sb("mask", [P, GRID_W])
        slab = m.sb("slab", [P, DR, GRID_W])
        sq = m.sb("sq", [P, TC])
        root = m.sb("root", [P, TC])
        rstd = m.sb("rstd", [P, TC])
        q = m.sb("q", [P, ROWS, P])
        k_t = m.sb("k_t", [P, TC])
        v = m.sb("v", [P, VT, P])
        v_odd = m.sb("v_odd", [P, VS, P])
        s = m.sb("s", [P, 2, KEYS])
        p = m.sb("p", [P, 2, ALL])
        p_t = m.sb("p_t", [P, 2, NT, P])
        stat = m.sb("stat", [P, 2, 8])
        o = m.sb("o", [P, T])
        ps_a = m.ps("ps_a", [P, 3 * HALF])
        ps_b = m.ps("ps_b", [P, 3 * HALF])
        ps_t = m.ps("ps_t", [P, 2 * HALF])
        score = [ps_a, ps_b]
        consts_in, q_in, k_in, slab_in, v_in = (m.sem(x) for x in ("consts_in", "q_in", "k_in", "slab_in", "v_in"))
        hi_done, lo_done, proj_done, sq_done, sum_done, root_done = (m.sem(x) for x in (
            "hi_done", "lo_done", "proj_done", "sq_done", "sum_done", "root_done"))
        consts, rstd_done, q_done, k_done, slab_done = (m.sem(x) for x in ("consts", "rstd_done", "q_done", "k_done", "slab_done"))
        s_ready, row_max, row_stat, exp_done, p_norm, p_ready = (m.sem(x) for x in (
            "s_ready", "row_max", "row_stat", "exp_done", "p_norm", "p_ready"))
        t_ready, t_copied, o_ready, o_copied, o_stored = (m.sem(x) for x in ("t_ready", "t_copied", "o_ready", "o_copied", "o_stored"))
        block = ctx.enter_context(nc.Block())

        @block.sync
        def _(sp):
            sp.dma_start(qk_w[:], io["qk_w"]).then_inc(consts_in, 16)
            sp.dma_start(mask[:], io["mask"]).then_inc(consts_in, 16)
            sp.dma_start(ident[:], io["ident"]).then_inc(consts_in, 16)
            sp.dma_start(head_ones[:], io["head_ones"]).then_inc(consts_in, 16)
            with sp.Fori(0, PAIRS) as h:
                v_col = sp.snap(h * P)
                sp.wait_ge(lo_done, 2 * h)
                sp.dma_start(raw[:, 0], io["w_q"][h].rearrange("p (k n) -> p k n", k=KD)).then_inc(q_in, 16)
                sp.dma_start(raw[:, 1], io["w_k"][h].rearrange("p (k n) -> p k n", k=KD)).then_inc(k_in, 16)
                sp.wait_ge(row_max, ROWS * h)
                sp.dma_start(slab[:], io["rpb"][h].rearrange("p (d c) -> p d c", d=DR)).then_inc(slab_in, 16)
                sp.wait_ge(o_ready, ROWS * h)
                sp.dma_start(v[:], io["v_scr"][:, bass.ds(v_col, P)].rearrange("(j p) c -> p j c", p=P)).then_inc(v_in, 16)
                sp.dma_start(v_odd[:], io["v_scr"][GRID_W:GRID_W + VS * P, bass.ds(v_col, P)].rearrange("(j p) c -> p j c", p=P))\
                    .then_inc(v_in, 16)
                sp.wait_ge(o_copied, ROWS * (h + 1))
                sp.dma_start(io["oa_scr"][h], o[:]).then_inc(o_stored, 16)
            sp.wait_ge(o_stored, 16 * PAIRS)

        @block.scalar
        def _(act):
            act.wait_ge(consts, 1)
            with act.Fori(0, PAIRS) as h:
                act.wait_ge(q_in, 16 * (h + 1))
                nc.scalar.activation(w_hi[:, 0], raw[:, 0], ACT.Copy).then_inc(hi_done, 1)
                act.wait_ge(k_in, 16 * (h + 1))
                nc.scalar.activation(w_hi[:, 1], raw[:, 1], ACT.Copy).then_inc(hi_done, 1)
                act.wait_ge(proj_done, 2 * h + 1)
                nc.scalar.activation(sq[:, 0:T], ps_a[:, 0:T], ACT.Square).then_inc(sq_done, 1)
                act.wait_ge(sum_done, 2 * h + 1)
                nc.scalar.activation(root[:, 0:T], ps_t[:], ACT.Sqrt, bias=eps[:], scale=1.0 / HD).then_inc(root_done, 1)
                act.wait_ge(proj_done, 2 * h + 2)
                nc.scalar.activation(sq[:], ps_b[:, 0:TC], ACT.Square).then_inc(sq_done, 1)
                act.wait_ge(sum_done, 2 * h + 2)
                act.wait_ge(rstd_done, 2 * h + 1)
                nc.scalar.activation(root[:], ps_a[:, 0:TC], ACT.Sqrt, bias=eps[:], scale=1.0 / HD).then_inc(root_done, 1)
                for i in range(ROWS + 2):
                    if i < ROWS:
                        g, b = ROWS * h + i, i % 2
                        act.wait_ge(row_max, g + 1)
                        if i >= 2:
                            act.wait_ge(t_ready, g - 1)
                        nc.scalar.activation(p[:, b, 0:KEYS], s[:, b], ACT.Exp, bias=stat[:, b, 2:3], accum_out=stat[:, b, 3:4])
                        nc.scalar.activation(p[:, b, KEYS:ALL], score[b][:, KEYS:ALL], ACT.Exp, bias=stat[:, b, 2:3],
                                             accum_out=stat[:, b, 4:5]).then_inc(exp_done, 1)
                    if i >= 2:
                        r = i - 2
                        act.wait_ge(t_ready, ROWS * h + r + 1)
                        if r >= 2:
                            act.wait_ge(o_ready, ROWS * h + r - 1)
                        nc.scalar.activation(p_t[:, r % 2], ps_t[:, 0:ALL].rearrange("p (j n) -> p j n", j=NT), ACT.Copy)\
                            .then_inc(t_copied, 1)

        @block.vector
        def _(dve):
            nc.vector.memset(eps[:], EPS).then_inc(consts, 1)
            nc.vector.memset(q[:], 0.0).then_inc(consts, 1)
            dve.wait_ge(consts_in, 64)
            nc.vector.tensor_scalar_mul(q_w[:], qk_w[:, 0:1], SCALE).then_inc(consts, 1)
            dve.wait_ge(consts, 3)
            with dve.Fori(0, PAIRS) as h:
                for u in range(2):
                    dve.wait_ge(hi_done, 2 * h + u + 1)
                    nc.vector.tensor_tensor(w_lo[:, u], raw[:, u], w_hi[:, u].bitcast(F32), ALU.subtract).then_inc(lo_done, 1)
                dve.wait_ge(slab_in, 16 * (h + 1))
                nc.vector.tensor_tensor(slab[:], slab[:], mask[:].rearrange("p (a c) -> p a c", a=1).broadcast_to([P, DR, GRID_W]), ALU.add)\
                    .then_inc(slab_done, 1)
                dve.wait_ge(root_done, 2 * h + 1)
                nc.vector.reciprocal(rstd[:, 0:T], root[:, 0:T]).then_inc(rstd_done, 1)
                dve.wait_ge(rstd_done, 2 * h + 1)
                for a in range(2):
                    half = slice(a * HD, (a + 1) * HD)
                    nc.vector.scalar_tensor_tensor(
                        out=q[half, :, half], in0=ps_a[half, 0:T].rearrange("p (r c) -> p r c", r=ROWS), scalar=q_w[half],
                        in1=rstd[half, 0:T].rearrange("p (r c) -> p r c", r=ROWS), op0=ALU.mult, op1=ALU.mult).then_inc(q_done, 1)
                dve.wait_ge(root_done, 2 * h + 2)
                dve.wait_ge(q_done, 2 * h + 2)
                nc.vector.reciprocal(rstd[:], root[:]).then_inc(rstd_done, 1)
                dve.wait_ge(rstd_done, 2 * h + 2)
                nc.vector.scalar_tensor_tensor(out=k_t[:], in0=ps_b[:, 0:TC], scalar=qk_w[:, 1:2], in1=rstd[:],
                                               op0=ALU.mult, op1=ALU.mult).then_inc(k_done, 1)
                dve.wait_ge(slab_done, h + 1)
                dve.wait_ge(o_stored, 16 * h)
                for i in range(ROWS + 3):
                    if i < ROWS:
                        g, b = ROWS * h + i, i % 2
                        dve.wait_ge(s_ready, g + 1)
                        if i >= 2:
                            dve.wait_ge(exp_done, g - 1)
                            dve.wait_ge(p_ready, g - 1)
                        d0 = row0[i] - i + WIN - 1
                        nc.vector.reduce_max(stat[:, b, 1:2], score[b][:, KEYS:ALL], AX_X).then_inc(row_stat, 1)
                        nc.vector.tensor_tensor_reduce(
                            out=s[:, b], in0=score[b][:, 0:KEYS], in1=slab[:, d0:d0 + WIN].rearrange("p d c -> p (d c)"), scale=1.0,
                            scalar=-3e38, op0=ALU.add, op1=ALU.max, accum_out=stat[:, b, 0:1]).then_inc(row_stat, 1)
                        dve.wait_ge(row_stat, 2 * g + 2)
                        nc.vector.tensor_scalar(stat[:, b, 2:3], stat[:, b, 0:1], stat[:, b, 1:2], -1.0, ALU.max, ALU.mult)\
                            .then_inc(row_max, 1)
                    if 1 <= i <= ROWS:
                        r = i - 1
                        g, b = ROWS * h + r, r % 2
                        dve.wait_ge(exp_done, g + 1)
                        nc.vector.tensor_tensor(stat[:, b, 5:6], stat[:, b, 3:4], stat[:, b, 4:5], ALU.add).then_inc(p_norm, 1)
                        dve.wait_ge(p_norm, 2 * g + 1)
                        nc.vector.reciprocal(stat[:, b, 6:7], stat[:, b, 5:6]).then_inc(p_norm, 1)
                        dve.wait_ge(p_norm, 2 * g + 2)
                        nc.vector.tensor_scalar(p[:, b], p[:, b], stat[:, b, 6:7], None, ALU.mult).then_inc(p_ready, 1)
                    if i >= 3:
                        r = i - 3
                        dve.wait_ge(o_ready, ROWS * h + r + 1)
                        ps_o = score[r % 2][:, 2 * HALF:2 * HALF + P]
                        cols = slice(r * GRID_W, (r + 1) * GRID_W)
                        nc.vector.tensor_copy(o[0:HD, cols], ps_o[0:HD, 0:HD])
                        nc.vector.tensor_copy(o[HD:P, cols], ps_o[HD:P, HD:P]).then_inc(o_copied, 1)

        @block.tensor
        def _(pe):
            pe.wait_ge(consts_in, 64)
            with pe.Fori(0, PAIRS) as h:
                pe.wait_ge(o_copied, ROWS * h)
                for u, (out, n) in enumerate(((ps_a, T), (ps_b, TC))):
                    pe.wait_ge(lo_done, 2 * h + u + 1)
                    for k in range(KD):
                        for a, b in split_columns(n):
                            last = product3(nc, out[:, a:b], w_hi[:, u, k], w_lo[:, u, k], keep.h_hi.at(k, a, b), keep.h_lo.at(k, a, b),
                                            k == 0, k == KD - 1)
                    last.then_inc(proj_done, 1)
                pe.wait_ge(sq_done, 2 * h + 1)
                for a, b in split_columns(T):
                    last = nc.tensor.matmul(ps_t[:, a:b], head_ones[:], sq[:, a:b], start=True, stop=True)
                last.then_inc(sum_done, 1)
                pe.wait_ge(sq_done, 2 * h + 2)
                pe.wait_ge(q_done, 2 * h + 2)
                for a, b in split_columns(TC):
                    last = nc.tensor.matmul(ps_a[:, a:b], head_ones[:], sq[:, a:b], start=True, stop=True)
                last.then_inc(sum_done, 1)
                pe.wait_ge(k_done, h + 1)
                pe.wait_ge(v_in, 32 * (h + 1))
                for i in range(ROWS + 3):
                    if i < ROWS:
                        b = i % 2
                        if i >= 2:
                            pe.wait_ge(exp_done, ROWS * h + i - 1)
                        w0 = row0[i] * GRID_W
                        nc.tensor.matmul(score[b][:, 0:KEYS], q[:, i], k_t[:, w0:w0 + KEYS], start=True, stop=True)
                        nc.tensor.matmul(score[b][:, KEYS:ALL], q[:, i], k_t[:, T:TC], start=True, stop=True).then_inc(s_ready, 1)
                    if 2 <= i < ROWS + 2:
                        r = i - 2
                        pe.wait_ge(p_ready, ROWS * h + r + 1)
                        pe.wait_ge(t_copied, ROWS * h + r)
                        for j in range(NT):
                            last = nc.tensor.transpose(ps_t[:, j * P:(j + 1) * P], p[:, r % 2, j * P:(j + 1) * P], ident[:])
                        last.then_inc(t_ready, 1)
                    if i >= 3:
                        r = i - 3
                        pe.wait_ge(t_copied, ROWS * h + r + 1)
                        if r >= 2:
                            pe.wait_ge(o_copied, ROWS * h + r - 1)
                        tiles = v if row0[r] % 2 == 0 else v_odd
                        ps_o = score[r % 2][:, 2 * HALF:2 * HALF + P]
                        for j in range(NT):
                            v_tile = tiles[:, row0[r] // 2 + j] if j < KEYS // P else v[:, T // P + j - KEYS // P]
                            last = nc.tensor.matmul(ps_o, v_tile, p_t[:, r % 2, j], start=(j == 0), stop=(j == NT - 1))
                        last.then_inc(o_ready, 1)


CONV_W, CONV_B, BIAS, LAM = 0, 4, 5, 9
HALF_BIAS, NEG_C, HALF_C = 0, 4, 6
NVEC, NDER = 11, 8
LOG1P_TERMS = 9


def recurrence(nc, io, keep):
    GAP = CONV - 1
    U_CTX = T + GAP
    UW = U_CTX + C + 1
    ZW = UW + GAP
    with ExitStack() as ctx:
        m = Pool(nc, ctx, "r")
        raw = m.sb("raw", [P, 2, KD, P])
        w_hi = m.sb("w_hi", [P, 2, KD, P], F32R)
        w_lo = m.sb("w_lo", [P, 2, KD, P], F32R)
        gate_w = m.sb("gate_w", [P, 4, P])
        vec = m.sb("vec", [P, BLOCKS, NVEC])
        der = m.sb("der", [P, BLOCKS, NDER])
        sp_t = m.sb("sp_t", [P, 6, BLOCKS, 2])
        z = m.sb("z", [P, ZW])
        u = m.sb("u", [P, UW])
        tr = m.sb("tr", [P, 2, UW])
        ti = m.sb("ti", [P, 2, UW])
        a = m.sb("a", [P, 2, UW])
        root = m.sb("root", [P, 2, UW])
        hs = m.sb("hs", [P, 2, UW])
        gy = m.sb("gy", [P, T])
        ob = m.sb("ob", [P, T])
        ps = [m.ps("ps_a", [P, 3 * HALF]), m.ps("ps_b", [P, 3 * HALF])]
        ps_y = m.ps("ps_y", [P, T])
        vec_in, x_in, y_in, gate_in, stored = (m.sem(x) for x in ("vec_in", "x_in", "y_in", "gate_in", "stored"))
        hi_done, lo_done, x_done, y_done, g_done = (m.sem(x) for x in ("hi_done", "lo_done", "x_done", "y_done", "g_done"))
        pads, lam_abs, lam_exp, lam_step, der_done = (m.sem(x) for x in ("pads", "lam_abs", "lam_exp", "lam_step", "der_done"))
        z_done, conv_step, tanh_done, a_done, t_done, root_done, gelu_done = (m.sem(x) for x in (
            "z_done", "conv_step", "tanh_done", "a_done", "t_done", "root_done", "gelu_done"))
        iu_done, beta_done, b_done, scan_done, sum_done, ob_done = (m.sem(x) for x in (
            "iu_done", "beta_done", "b_done", "scan_done", "sum_done", "ob_done"))
        block = ctx.enter_context(nc.Block())

        def load_weights(sp, n):
            sp.dma_start(raw[:, 0], io["w_xr"][n].rearrange("p (k n) -> p k n", k=KD)).then_inc(x_in, 16)
            sp.dma_start(raw[:, 1], io["w_yr"][n].rearrange("p (k n) -> p k n", k=KD)).then_inc(y_in, 16)

        @block.sync
        def _(sp):
            sp.dma_start(vec[:], io["lru_vec"].rearrange("p (n v) -> p n v", n=BLOCKS)).then_inc(vec_in, 16)
            load_weights(sp, 0)
            with sp.Fori(0, BLOCKS) as n:
                sp.wait_ge(lo_done, 2 * n + 2)
                load_weights(sp, n + 1)
                sp.wait_ge(g_done, 4 * n)
                sp.dma_start(gate_w[:], io["w_gates"][n].rearrange("p (g n) -> p g n", g=4)).then_inc(gate_in, 16)
                sp.wait_ge(ob_done, n + 1)
                sp.dma_start(io["ob_scr"][n], ob[:]).then_inc(stored, 16)
            sp.wait_ge(stored, 16 * BLOCKS)
            sp.wait_ge(x_in, 16 * (BLOCKS + 1))
            sp.wait_ge(y_in, 16 * (BLOCKS + 1))

        @block.scalar
        def _(act):
            act.wait_ge(lam_abs, 1)
            nc.scalar.activation(sp_t[:, 1], sp_t[:, 0], ACT.Exp, scale=-1.0).then_inc(lam_exp, 1)
            act.wait_ge(x_in, 16)
            nc.scalar.activation(w_hi[:, 0], raw[:, 0], ACT.Copy).then_inc(hi_done, 1)
            act.wait_ge(y_in, 16)
            nc.scalar.activation(w_hi[:, 1], raw[:, 1], ACT.Copy).then_inc(hi_done, 1)
            act.wait_ge(der_done, 3)
            act.wait_ge(pads, 1)
            with act.Fori(0, BLOCKS) as n:
                act.wait_ge(x_done, n + 1)
                act.wait_ge(conv_step, 4 * n)
                nc.scalar.activation(z[:, CONV_LEFT:CONV_LEFT + T], ps[0][:, 0:T], ACT.Copy)
                nc.scalar.activation(z[:, U_CTX + CONV_LEFT:U_CTX + CONV_LEFT + C], ps[0][:, T:TC], ACT.Copy).then_inc(z_done, 1)
                act.wait_ge(x_in, 16 * (n + 2))
                nc.scalar.activation(w_hi[:, 0], raw[:, 0], ACT.Copy).then_inc(hi_done, 1)
                act.wait_ge(y_in, 16 * (n + 2))
                act.wait_ge(y_done, n + 1)
                nc.scalar.activation(w_hi[:, 1], raw[:, 1], ACT.Copy).then_inc(hi_done, 1)
                act.wait_ge(b_done, 2 * n)
                for j in range(4):
                    d, which = j // 2, (tr, ti)[j % 2]
                    act.wait_ge(g_done, 4 * n + j + 1)
                    nc.scalar.activation(which[:, d], ps[(j + 1) % 2][:, 0:UW], ACT.Tanh, scale=0.5,
                                         bias=der[:, bass.ds(n, 1), HALF_BIAS + j].rearrange("p a -> p a")).then_inc(tanh_done, 1)
                act.wait_ge(scan_done, 4 * n)
                for d in range(2):
                    act.wait_ge(tanh_done, 4 * n + 2 * d + 1)
                    c = der[:, bass.ds(n, 1), NEG_C + d]
                    nc.scalar.activation(a[:, d], tr[:, d], ACT.Exp, scale=c, bias=c).then_inc(a_done, 1)
                    c = der[:, bass.ds(n, 1), HALF_C + d]
                    nc.scalar.activation(root[:, d], tr[:, d], ACT.Tanh, scale=c, bias=c).then_inc(t_done, 1)
                for d in range(2):
                    act.wait_ge(t_done, 2 * n + d + 1)
                    nc.scalar.activation(root[:, d], root[:, d], ACT.Sqrt, scale=0.25).then_inc(root_done, 1)
                act.wait_ge(ob_done, n)
                nc.scalar.activation(gy[:], ps_y[:], ACT.Gelu_apprx_tanh).then_inc(gelu_done, 1)

        @block.vector
        def _(dve):
            nc.vector.memset(z[:], 0.0).then_inc(pads, 1)
            dve.wait_ge(vec_in, 16)
            nlam, e, den, q, acc, rest = (sp_t[:, i] for i in range(6))
            lam = vec[:, :, LAM:LAM + 2]
            steps = 0

            def step(instruction):
                nonlocal steps
                steps += 1
                instruction.then_inc(lam_step, 1)
                dve.wait_ge(lam_step, steps)
            step(nc.vector.tensor_scalar_mul(rest, lam, -1.0))
            nc.vector.tensor_tensor(nlam, lam, rest, ALU.max).then_inc(lam_abs, 1)
            dve.wait_ge(lam_exp, 1)
            step(nc.vector.tensor_scalar_add(den, e, 2.0))
            step(nc.vector.reciprocal(den, den))
            step(nc.vector.tensor_tensor(e, e, den, ALU.mult))
            step(nc.vector.tensor_tensor(q, e, e, ALU.mult))
            step(nc.vector.memset(acc, 1.0 / (2 * LOG1P_TERMS + 1)))
            for t in reversed(range(LOG1P_TERMS)):
                step(nc.vector.tensor_tensor(acc, acc, q, ALU.mult))
                step(nc.vector.tensor_scalar_add(acc, acc, 1.0 / (2 * t + 1)))
            step(nc.vector.tensor_tensor(acc, acc, e, ALU.mult))
            step(nc.vector.tensor_scalar_mul(acc, acc, 2.0))
            step(nc.vector.tensor_scalar_max(rest, rest, 0.0))
            step(nc.vector.tensor_tensor(acc, acc, rest, ALU.add))
            nc.vector.tensor_scalar_mul(der[:, :, NEG_C:NEG_C + 2], acc, -4.0).then_inc(der_done, 1)
            nc.vector.tensor_scalar_mul(der[:, :, HALF_C:HALF_C + 2], acc, 2.0).then_inc(der_done, 1)
            nc.vector.tensor_scalar_mul(der[:, :, HALF_BIAS:HALF_BIAS + 4], vec[:, :, BIAS:BIAS + 4], 0.5).then_inc(der_done, 1)
            for h in range(2):
                dve.wait_ge(hi_done, h + 1)
                nc.vector.tensor_tensor(w_lo[:, h], raw[:, h], w_hi[:, h].bitcast(F32), ALU.subtract).then_inc(lo_done, 1)
            with dve.Fori(0, BLOCKS) as n:
                dve.wait_ge(z_done, n + 1)
                dve.wait_ge(g_done, 4 * n)
                dve.wait_ge(iu_done, 2 * n)
                nc.vector.tensor_scalar(u[:], z[:, 0:UW], vec[:, bass.ds(n, 1), CONV_W], vec[:, bass.ds(n, 1), CONV_B], ALU.mult, ALU.add)\
                    .then_inc(conv_step, 1)
                for j in range(1, CONV):
                    dve.wait_ge(conv_step, 4 * n + j)
                    nc.vector.scalar_tensor_tensor(out=u[:], in0=z[:, j:j + UW], scalar=vec[:, bass.ds(n, 1), CONV_W + j], in1=u[:],
                                                   op0=ALU.mult, op1=ALU.add).then_inc(conv_step, 1)
                for h in range(2):
                    dve.wait_ge(hi_done, 2 * n + 3 + h)
                    nc.vector.tensor_tensor(w_lo[:, h], raw[:, h], w_hi[:, h].bitcast(F32), ALU.subtract).then_inc(lo_done, 1)
                for d in range(2):
                    dve.wait_ge(tanh_done, 4 * n + 2 * d + 2)
                    nc.vector.scalar_tensor_tensor(out=ti[:, d], in0=ti[:, d], scalar=1.0, in1=u[:], op0=ALU.add, op1=ALU.mult)\
                        .then_inc(iu_done, 1)
                for d in range(2):
                    dve.wait_ge(root_done, 2 * n + d + 1)
                    nc.vector.scalar_tensor_tensor(out=root[:, d], in0=a[:, d], scalar=1.0, in1=root[:, d], op0=ALU.add, op1=ALU.mult)\
                        .then_inc(beta_done, 1)
                for d in range(2):
                    dve.wait_ge(beta_done, 2 * n + d + 1)
                    dve.wait_ge(iu_done, 2 * n + d + 1)
                    nc.vector.tensor_tensor(ti[:, d], ti[:, d], root[:, d], ALU.mult).then_inc(b_done, 1)
                dve.wait_ge(sum_done, n)
                lat, con = slice(0, T), slice(U_CTX, U_CTX + C)
                for d, (order, end) in enumerate(((1, U_CTX + C - 1), (-1, U_CTX))):
                    dve.wait_ge(b_done, 2 * n + d + 1)
                    nc.vector.tensor_tensor_scan(hs[:, d, con][:, ::order], a[:, d, con][:, ::order], ti[:, d, con][:, ::order], 0.0,
                                                 ALU.mult, ALU.add).then_inc(scan_done, 1)
                    dve.wait_ge(scan_done, 4 * n + 2 * d + 1)
                    nc.vector.tensor_tensor_scan(hs[:, d, lat][:, ::order], a[:, d, lat][:, ::order], ti[:, d, lat][:, ::order],
                                                 hs[:, d, end:end + 1], ALU.mult, ALU.add).then_inc(scan_done, 1)
                dve.wait_ge(scan_done, 4 * n + 4)
                dve.wait_ge(stored, 16 * n)
                nc.vector.tensor_tensor(ob[:], hs[:, 0, lat], hs[:, 1, lat], ALU.add).then_inc(sum_done, 1)
                dve.wait_ge(gelu_done, n + 1)
                dve.wait_ge(sum_done, n + 1)
                nc.vector.tensor_tensor(ob[:], ob[:], gy[:], ALU.mult).then_inc(ob_done, 1)

        @block.tensor
        def _(pe):
            with pe.Fori(0, BLOCKS) as n:
                pe.wait_ge(tanh_done, 4 * n)
                for h, (out, width, done) in enumerate(((ps[0], TC, x_done), (ps_y, T, y_done))):
                    pe.wait_ge(lo_done, 2 * n + h + 1)
                    if h == 1:
                        pe.wait_ge(gelu_done, n)
                    for k in range(KD):
                        for c0, c1 in split_columns(width):
                            last = product3(nc, out[:, c0:c1], w_hi[:, h, k], w_lo[:, h, k], keep.h_hi.at(k, c0, c1), keep.h_lo.at(k, c0, c1),
                                            k == 0, k == KD - 1)
                    last.then_inc(done, 1)
                pe.wait_ge(gate_in, 16 * (n + 1))
                pe.wait_ge(conv_step, 4 * (n + 1))
                for j in range(4):
                    if j >= 2:
                        pe.wait_ge(tanh_done, 4 * n + j - 1)
                    for c0, c1 in split_columns(UW):
                        last = nc.tensor.matmul(ps[(j + 1) % 2][:, c0:c1], gate_w[:, j], u[:, c0:c1], start=True, stop=True)
                    last.then_inc(g_done, 1)


def merge(nc, io, keep):
    with ExitStack() as ctx:
        m = Pool(nc, ctx, "m")
        oa_hi, oa_lo = (m.sb(x, [P, PAIRS, T], F32R) for x in ("oa_hi", "oa_lo"))
        ob_hi, ob_lo = (m.sb(x, [P, BLOCKS, T], F32R) for x in ("ob_hi", "ob_lo"))
        raw = m.sb("raw", [P, 2, KD * P])
        w_hi = m.sb("w_hi", [P, 2, KD, P], F32R)
        w_lo = m.sb("w_lo", [P, 2, KD, P], F32R)
        part = m.sb("part", [P, 2, T])
        mg = m.sb("mg", [P, T])
        acc = m.ps("acc", [P, 4, T])
        raw_in = [m.sem(f"raw_in{b}") for b in range(2)]
        hi_done, lo_done, prod_done, sig_done, part_done, mg_done, stored = (m.sem(x) for x in (
            "hi_done", "lo_done", "prod_done", "sig_done", "part_done", "mg_done", "stored"))
        block = ctx.enter_context(nc.Block())
        pieces = [("oa_scr", i, oa_hi, oa_lo) for i in range(PAIRS)] + [("ob_scr", i, ob_hi, ob_lo) for i in range(BLOCKS)]
        NP = len(pieces)
        GROUPS = (("w_ga", KD), ("w_gb", KD), ("w_oa", PAIRS), ("w_ol", KD))

        @block.sync
        def _(sp):
            for n, (name, i, _, _) in enumerate(pieces):
                if n >= 2:
                    sp.wait_ge(lo_done, n - 1)
                sp.dma_start(raw[:, n % 2], io[name][i]).then_inc(raw_in[n % 2], 16)
            with sp.Fori(0, KD) as i:
                for g, (name, kd) in enumerate(GROUPS):
                    sp.wait_ge(lo_done, 4 * i + (NP - 1 + g))
                    sp.dma_start(raw[:, g % 2, 0:kd * P], io[name][i]).then_inc(raw_in[g % 2], 16)
                sp.wait_ge(mg_done, i + 1)
                sp.dma_start(io["mg_scr"][i], mg[:]).then_inc(stored, 16)
            sp.wait_ge(stored, 16 * KD)

        @block.scalar
        def _(act):
            for n, (_, i, hi, _) in enumerate(pieces):
                act.wait_ge(raw_in[n % 2], 16 * (n // 2 + 1))
                nc.scalar.activation(hi[:, i], raw[:, n % 2], ACT.Copy).then_inc(hi_done, 1)
            with act.Fori(0, KD) as i:
                for g, (_, kd) in enumerate(GROUPS):
                    act.wait_ge(raw_in[g % 2], 32 * i + 16 * (NP // 2 + g // 2 + 1))
                    if g >= 2:
                        act.wait_ge(prod_done, 4 * i + g - 1)
                    else:
                        act.wait_ge(prod_done, 4 * i)
                    nc.scalar.activation(w_hi[:, g % 2, 0:kd], raw[:, g % 2, 0:kd * P].rearrange("p (k n) -> p k n", n=P), ACT.Copy)\
                        .then_inc(hi_done, 1)
                    if g == 1:
                        act.wait_ge(part_done, 2 * i)
                    if g >= 2:
                        act.wait_ge(prod_done, 4 * i + g - 1)
                        nc.scalar.activation(part[:, g - 2], acc[:, g - 2], ACT.Sigmoid).then_inc(sig_done, 1)

        @block.vector
        def _(dve):
            for n, (_, i, hi, lo) in enumerate(pieces):
                dve.wait_ge(hi_done, n + 1)
                nc.vector.tensor_tensor(lo[:, i], raw[:, n % 2], hi[:, i].bitcast(F32), ALU.subtract).then_inc(lo_done, 1)
            with dve.Fori(0, KD) as i:
                for g, (_, kd) in enumerate(GROUPS):
                    dve.wait_ge(hi_done, 4 * i + NP + g + 1)
                    nc.vector.tensor_tensor(w_lo[:, g % 2, 0:kd], raw[:, g % 2, 0:kd * P].rearrange("p (k n) -> p k n", n=P),
                                            w_hi[:, g % 2, 0:kd].bitcast(F32), ALU.subtract).then_inc(lo_done, 1)
                for b in range(2):
                    dve.wait_ge(prod_done, 4 * i + b + 3)
                    dve.wait_ge(sig_done, 2 * i + b + 1)
                    nc.vector.tensor_tensor(part[:, b], part[:, b], acc[:, 2 + b], ALU.mult).then_inc(part_done, 1)
                dve.wait_ge(part_done, 2 * i + 2)
                dve.wait_ge(stored, 16 * i)
                nc.vector.tensor_tensor(mg[:], part[:, 0], part[:, 1], ALU.add).then_inc(mg_done, 1)

        @block.tensor
        def _(pe):
            with pe.Fori(0, KD) as i:
                for g, (_, kd) in enumerate(GROUPS):
                    pe.wait_ge(lo_done, 4 * i + NP + g + 1)
                    if g < 2:
                        pe.wait_ge(sig_done, 2 * i)
                    else:
                        pe.wait_ge(part_done, 2 * i)
                    for k in range(kd):
                        for a, b in split_columns(T):
                            if g < 2:
                                hi, lo = keep.h_hi.at(k, a, b), keep.h_lo.at(k, a, b)
                            elif g == 2:
                                hi, lo = oa_hi[:, k, a:b], oa_lo[:, k, a:b]
                            else:
                                hi, lo = ob_hi[:, k, a:b], ob_lo[:, k, a:b]
                            last = product3(nc, acc[:, g, a:b], w_hi[:, g % 2, k], w_lo[:, g % 2, k], hi, lo, k == 0, k == kd - 1)
                    last.then_inc(prod_done, 1)


def project(nc, io, keep):
    with ExitStack() as ctx:
        m = Pool(nc, ctx, "p")
        mg_hi, mg_lo = (m.sb(x, [P, KD, T], F32R) for x in ("mg_hi", "mg_lo"))
        raw = m.sb("raw", [P, 2, KD * P])
        w_hi = m.sb("w_hi", [P, 2, KD, P], F32R)
        w_lo = m.sb("w_lo", [P, 2, KD, P], F32R)
        x = m.sb("x", [P, 2, T])
        x1 = m.sb("x1", [P, KD, T])
        ones = m.sb("ones", [P, P])
        eps = m.sb("eps", [P, 1])
        acc = m.ps("acc", [P, 2, T])
        ps_sum = m.ps("ps_sum", [P, T])
        raw_in = [m.sem(f"raw_in{b}") for b in range(2)]
        x_in = [m.sem(f"x_in{b}") for b in range(2)]
        hi_done, lo_done, prod_done, x1_done, stored = (m.sem(s) for s in ("hi_done", "lo_done", "prod_done", "x1_done", "stored"))
        consts, sq_done, sq_summed, root_done, rstd_done, normed, modulated, h2_hi_done, h2_lo_done = (m.sem(s) for s in (
            "consts", "sq_done", "sq_summed", "root_done", "rstd_done", "normed", "modulated", "h2_hi_done", "h2_lo_done"))
        block = ctx.enter_context(nc.Block())

        @block.sync
        def _(sp):
            for n in range(KD):
                if n >= 2:
                    sp.wait_ge(lo_done, n - 1)
                sp.dma_start(raw[:, n % 2], io["mg_scr"][n]).then_inc(raw_in[n % 2], 16)
            with sp.Fori(0, KD // 2) as i:
                for b in range(2):
                    sp.wait_ge(lo_done, 2 * i + (KD - 1 + b))
                    sp.dma_start(raw[:, b], io["w_out"][2 * i + b]).then_inc(raw_in[b], 16)
                    x_col = sp.snap((2 * i + b) * T)
                    sp.wait_ge(x1_done, 2 * i + b + 1)
                    sp.dma_start(x[:, b], io["xt"][:, bass.ds(x_col, T)]).then_inc(x_in[b], 16)
            for n in range(KD):
                sp.wait_ge(x1_done, 2 + n + 1)
                sp.dma_start(io["x1_scr"][n], x1[:, n]).then_inc(stored, 16)
            sp.wait_ge(stored, 16 * KD)

        @block.scalar
        def _(act):
            for n in range(KD):
                act.wait_ge(raw_in[n % 2], 16 * (n // 2 + 1))
                nc.scalar.activation(mg_hi[:, n], raw[:, n % 2], ACT.Copy).then_inc(hi_done, 1)
            with act.Fori(0, KD // 2) as i:
                for b in range(2):
                    act.wait_ge(raw_in[b], 16 * i + 16 * (KD // 2 + 1))
                    act.wait_ge(prod_done, 2 * i + b + 1)
                    nc.scalar.activation(w_hi[:, b], raw[:, b].rearrange("p (k n) -> p k n", n=P), ACT.Copy).then_inc(hi_done, 1)
            act.wait_ge(x1_done, 2 + KD)
            for k in range(KD):
                if k >= 2:
                    act.wait_ge(sq_summed, k - 1)
                nc.scalar.activation(x[:, k % 2], x1[:, k], ACT.Square).then_inc(sq_done, 1)
            act.wait_ge(sq_summed, KD)
            nc.scalar.activation(x[:, 0], ps_sum[:], ACT.Sqrt, bias=eps[:], scale=1.0 / D).then_inc(root_done, 1)
            for k in range(KD):
                act.wait_ge(modulated, k + 1)
                nc.scalar.activation(keep.h2_hi[:, k], x1[:, k], ACT.Copy).then_inc(h2_hi_done, 1)

        @block.vector
        def _(dve):
            nc.vector.memset(ones[:], 1.0).then_inc(consts, 1)
            nc.vector.memset(eps[:], EPS).then_inc(consts, 1)
            dve.sem_inc(x1_done, 2)
            for n in range(KD):
                dve.wait_ge(hi_done, n + 1)
                nc.vector.tensor_tensor(mg_lo[:, n], raw[:, n % 2], mg_hi[:, n].bitcast(F32), ALU.subtract).then_inc(lo_done, 1)

            def split_weights(b, n):
                dve.wait_ge(hi_done, n + (KD + 1))
                nc.vector.tensor_tensor(w_lo[:, b], raw[:, b].rearrange("p (k n) -> p k n", n=P), w_hi[:, b].bitcast(F32), ALU.subtract)\
                    .then_inc(lo_done, 1)
            with dve.Fori(0, KD // 2) as i:
                for b in range(2):
                    split_weights(b, 2 * i + b)
                for b in range(2):
                    dve.wait_ge(prod_done, 2 * i + b + 3)
                    dve.wait_ge(x_in[b], 16 * (i + 1))
                    nc.vector.scalar_tensor_tensor(out=x1[:, bass.ds(2 * i + b, 1)], in0=acc[:, b:b + 1], scalar=keep.mod[:, bass.ds(2 * i + (2 * KD + b), 1)],
                                                   in1=x[:, b:b + 1], op0=ALU.mult, op1=ALU.add).then_inc(x1_done, 1)
            dve.wait_ge(root_done, 1)
            nc.vector.reciprocal(x[:, 1], x[:, 0]).then_inc(rstd_done, 1)
            dve.wait_ge(rstd_done, 1)
            dve.wait_ge(stored, 16 * KD)
            for k in range(KD):
                nc.vector.tensor_tensor(x1[:, k], x1[:, k], x[:, 1], ALU.mult).then_inc(normed, 1)
            for k in range(KD):
                dve.wait_ge(normed, k + 1)
                nc.vector.tensor_scalar(x1[:, k], x1[:, k], keep.gain[:, 2, k:k + 1], keep.mod[:, 3 * KD + k:3 * KD + k + 1],
                                        ALU.mult, ALU.add).then_inc(modulated, 1)
            for k in range(KD):
                dve.wait_ge(h2_hi_done, k + 1)
                nc.vector.tensor_tensor(keep.h2_lo[:, k], x1[:, k], keep.h2_hi[:, k].bitcast(F32), ALU.subtract).then_inc(h2_lo_done, 1)

        @block.tensor
        def _(pe):
            pe.sem_inc(prod_done, 2)
            with pe.Fori(0, KD // 2) as i:
                for b in range(2):
                    pe.wait_ge(lo_done, 2 * i + (KD + 1 + b))
                    pe.wait_ge(x1_done, 2 * i + b + 1)
                    for k in range(KD):
                        for c0, c1 in split_columns(T):
                            last = product3(nc, acc[:, b, c0:c1], w_hi[:, b, k], w_lo[:, b, k], mg_hi[:, k, c0:c1], mg_lo[:, k, c0:c1],
                                            k == 0, k == KD - 1)
                    last.then_inc(prod_done, 1)
            pe.wait_ge(consts, 2)
            for k in range(KD):
                pe.wait_ge(sq_done, k + 1)
                for c0, c1 in split_columns(T):
                    last = nc.tensor.matmul(ps_sum[:, c0:c1], ones[:], x[:, k % 2, c0:c1], start=(k == 0), stop=(k == KD - 1))
                last.then_inc(sq_summed, 1)


def hold(eng, semaphore, value, passed):
    eng.wait_ge(semaphore, value)
    eng.sem_inc(passed, 1)


USED = -3e38


def top16(nc, dve, n, values, scratch, best, place, done, base, passed):
    for i in range(n):
        nc.vector.max(best(i, 0), values(i)).then_inc(done, 1)
    hold(dve, done, base + n, passed)
    for i in range(n):
        nc.vector.match_replace(scratch(i), best(i, 0), values(i), USED).then_inc(done, 1)
    for i in range(n):
        nc.vector.max_index(place(i, 0), best(i, 0), values(i)).then_inc(done, 1)
    hold(dve, done, base + 2 * n, passed)
    for i in range(n):
        nc.vector.max(best(i, 1), scratch(i)).then_inc(done, 1)
    hold(dve, done, base + 4 * n, passed)
    for i in range(n):
        nc.vector.max_index(place(i, 1), best(i, 1), scratch(i)).then_inc(done, 1)


def route(nc, io, keep):
    UNITS = 2 * PH
    with ExitStack() as ctx:
        m = Pool(nc, ctx, "q")
        raw = m.sb("raw", [P, 2, KD, P])
        w_hi = m.sb("w_hi", [P, 2, KD, P], F32R)
        w_lo = m.sb("w_lo", [P, 2, KD, P], F32R)
        keys = m.sb("keys", [P, UNITS, NK])
        q = m.sb("q", [P, 2, T])
        struck = m.sb("struck", [P, TT, NK])
        best = m.sb("best", [P, TT, TOPK])
        place = m.sb("place", [P, TT, TOPK], U32)
        acc = m.ps("acc", [P, 2, T])
        score = m.ps("score", [P, 2, T])
        raw_in = [m.sem(f"raw_in{b}") for b in range(2)]
        keys_in, hi_done, lo_done, half_done, q_done, s_ready, top_done, kept, passed = (m.sem(x) for x in (
            "keys_in", "hi_done", "lo_done", "half_done", "q_done", "s_ready", "top_done", "kept", "passed"))
        block = ctx.enter_context(nc.Block())

        @block.sync
        def _(sp):
            sp.dma_start(keys[:], io["keys"].rearrange("p (u n) -> p u n", u=UNITS)).then_inc(keys_in, 16)
            with sp.Fori(0, UNITS // 2) as i:
                for b in range(2):
                    sp.wait_ge(lo_done, 2 * i + b + 1)
                    sp.dma_start(raw[:, b], io["w_pq"][2 * i + b].rearrange("p (k n) -> p k n", k=KD)).then_inc(raw_in[b], 16)
            sp.wait_ge(lo_done, UNITS + 1)
            sp.dma_start(raw[:, 0], io["w_pq"][UNITS].rearrange("p (k n) -> p k n", k=KD)).then_inc(raw_in[0], 16)

        @block.scalar
        def _(act):
            act.wait_ge(raw_in[0], 16)
            nc.scalar.activation(w_hi[:, 0], raw[:, 0], ACT.Copy).then_inc(hi_done, 1)
            with act.Fori(0, UNITS // 2) as i:
                for b in range(2):
                    nb = 1 - b
                    act.wait_ge(raw_in[nb], 16 * (i + 1 + b))
                    act.wait_ge(half_done, 4 * i + 2 * b)
                    nc.scalar.activation(w_hi[:, nb], raw[:, nb], ACT.Copy).then_inc(hi_done, 1)
                    act.wait_ge(s_ready, 2 * i + b)
                    for c, (c0, c1) in enumerate(split_columns(T)):
                        act.wait_ge(half_done, 4 * i + 2 * b + c + 1)
                        nc.scalar.activation(q[:, b, c0:c1], acc[:, b, c0:c1], ACT.Copy).then_inc(q_done, 1)

        @block.vector
        def _(dve):
            dve.sem_inc(lo_done, 2)
            dve.wait_ge(hi_done, 1)
            nc.vector.tensor_tensor(w_lo[:, 0], raw[:, 0], w_hi[:, 0].bitcast(F32), ALU.subtract).then_inc(lo_done, 1)
            with dve.Fori(0, UNITS // 2) as i:
                for b in range(2):
                    nb = 1 - b
                    dve.wait_ge(hi_done, 2 * i + b + 2)
                    nc.vector.tensor_tensor(w_lo[:, nb], raw[:, nb], w_hi[:, nb].bitcast(F32), ALU.subtract).then_inc(lo_done, 1)
                    hold(dve, kept, 4 * i + 2 * b, passed)
                    hold(dve, s_ready, 2 * i + b + 1, passed)
                    s = score[:, b].rearrange("p (t n) -> p t n", t=TT)
                    top16(nc, dve, TT, lambda t: s[:, t], lambda t: struck[:, t], lambda t, g: best[:, t, 8 * g:8 * g + 8],
                          lambda t, g: place[:, t, 8 * g:8 * g + 8], top_done, (2 * i + b) * (5 * TT), passed)
                    dve.wait_ge(top_done, (2 * i + b + 1) * (5 * TT))
                    unit = bass.ds(2 * i + b, 1)
                    nc.vector.tensor_copy(keep.best[:, :, unit], best[:].rearrange("p t (u n) -> p t u n", u=1)).then_inc(kept, 1)
                    nc.vector.tensor_copy(keep.place[:, :, unit], place[:].rearrange("p t (u n) -> p t u n", u=1)).then_inc(kept, 1)

        @block.tensor
        def _(pe):
            pe.wait_ge(keys_in, 16)
            with pe.Fori(0, UNITS // 2) as i:
                for b in range(2):
                    pe.wait_ge(lo_done, 2 * i + b + 3)
                    pe.wait_ge(q_done, 4 * i + 2 * b)
                    for c0, c1 in split_columns(T):
                        for k in range(KD):
                            last = product3(nc, acc[:, b, c0:c1], w_hi[:, b, k], w_lo[:, b, k], keep.h2_hi[:, k, c0:c1], keep.h2_lo[:, k, c0:c1],
                                            k == 0, k == KD - 1)
                        last.then_inc(half_done, 1)
                    pe.wait_ge(top_done, (2 * i + b) * (5 * TT))
                    for t in range(TT):
                        pe.wait_ge(q_done, 4 * i + 2 * b + t // (TT // 2) + 1)
                        last = nc.tensor.matmul(score[:, b, t * NK:(t + 1) * NK], q[:, b, t * P:(t + 1) * P],
                                                keys[:, bass.ds(2 * i + b, 1)].rearrange("p u n -> p (u n)"), start=True, stop=True)
                    last.then_inc(s_ready, 1)


def gates(nc, io, keep):
    SEL = PH * TOPK
    PAIRS2 = TOPK * TOPK
    GT = 8
    GROUPS = P // GT
    with ExitStack() as ctx:
        m = Pool(nc, ctx, "g")
        iota = m.sb("iota", [P, NK])
        ident = m.sb("ident", [P, P])
        va = m.sb("va", [P, 2 * PH, TOPK])
        xa = m.sb("xa", [P, 2 * PH, TOPK])
        cand = m.sb("cand", [P, PH, PAIRS2])
        struck = m.sb("struck", [P, PH, PAIRS2])
        best = m.sb("best", [P, PH, TOPK])
        pos = m.sb("pos", [P, SEL], U32)
        digit = m.sb("digit", [P, 2, SEL], U32)
        hit = m.sb("hit", [P, SEL, TOPK])
        total = m.sb("total", [P, PH])
        sel = m.sb("sel", [P, 3, SEL])
        sel_t = m.sb("sel_t", [P, 3, P])
        g_hi = m.sb("g_hi", [P, P], F32R)
        g_lo = m.sb("g_lo", [P, P])
        one2 = m.sb("one2", [P, 2, GT, NK], F32R)
        one1 = m.sb("one1", [P, 2, GT, 2, NK], F32R)
        gm = m.sb("gm", [P, NK, P])
        ps_t = m.ps("ps_t", [P, HALF])
        ps_g = m.ps("ps_g", [P, 2, GT * NK])
        consts_in, top_done, passed, step, sel_ready, exp_done, t_ready, oh_done, g_ready, g_copied, stored = (m.sem(x) for x in (
            "consts_in", "top_done", "passed", "step", "sel_ready", "exp_done", "t_ready", "oh_done", "g_ready", "g_copied", "stored"))
        STEPS = 18
        block = ctx.enter_context(nc.Block())

        @block.sync
        def _(sp):
            sp.dma_start(iota[:], io["iota"]).then_inc(consts_in, 16)
            sp.dma_start(ident[:], io["ident"]).then_inc(consts_in, 16)
            with sp.Fori(0, TT) as tt:
                col = sp.snap(tt * P)
                sp.wait_ge(g_copied, GROUPS * (tt + 1) + 2)
                sp.dma_start(io["gm_scr"][:, :, bass.ds(col, P)].rearrange("i p t -> p i t"), gm[:]).then_inc(stored, 16)
            sp.wait_ge(stored, 16 * TT)

        @block.scalar
        def _(act):
            act.sem_inc(g_copied, 2)
            with act.Fori(0, TT) as tt:
                act.wait_ge(step, STEPS * tt + 4)
                nc.scalar.activation(best[:], best[:], ACT.Exp).then_inc(exp_done, 1)
                act.wait_ge(stored, 16 * tt)
                with act.Fori(0, GROUPS // 2) as i:
                    for b in range(2):
                        act.wait_ge(g_ready, GROUPS * tt + 2 * i + b + 2)
                        nc.scalar.activation(gm[:, :, bass.ds(2 * GT * i + GT * b, GT)].rearrange("p i t -> p t i"),
                                             ps_g[:, b].rearrange("p (t i) -> p t i", t=GT), ACT.Copy).then_inc(g_copied, 1)

        @block.vector
        def _(dve):
            dve.wait_ge(consts_in, 32)
            with dve.Fori(0, TT) as tt:
                done = 0

                def then(instruction):
                    nonlocal done
                    done += 1
                    instruction.then_inc(step, 1)

                def ready(n=None):
                    dve.wait_ge(step, STEPS * tt + (done if n is None else n))

                then(nc.vector.tensor_copy(va[:], keep.best[:, bass.ds(tt, 1)].rearrange("p a u n -> p (a u) n")))
                then(nc.vector.tensor_copy(xa[:], keep.place[:, bass.ds(tt, 1)].rearrange("p a u n -> p (a u) n")))
                ready()
                v4 = va[:].rearrange("p (h s) k -> p h s k", s=2)
                x4 = xa[:].rearrange("p (h s) k -> p h s k", s=2)
                grid = [P, PH, TOPK, TOPK]
                then(nc.vector.tensor_tensor(
                    cand[:].rearrange("p h (a b) -> p h a b", a=TOPK), v4[:, :, 0].rearrange("p h (a o) -> p h a o", o=1).broadcast_to(grid),
                    v4[:, :, 1].rearrange("p h (o b) -> p h o b", o=1).broadcast_to(grid), ALU.add))
                hold(dve, step, STEPS * tt + done, passed)
                top16(nc, dve, PH, lambda h: cand[:, h], lambda h: struck[:, h], lambda h, g: best[:, h, 8 * g:8 * g + 8],
                      lambda h, g: pos[:, h * TOPK + 8 * g:h * TOPK + 8 * g + 8], top_done, tt * (5 * PH), passed)
                dve.wait_ge(top_done, (tt + 1) * (5 * PH))
                then(nc.vector.tensor_tensor(best[:], best[:], cand[:, :, 0:1].broadcast_to([P, PH, TOPK]), ALU.subtract))
                then(nc.vector.tensor_scalar(digit[:, 0], pos[:], 4, None, ALU.logical_shift_right))
                then(nc.vector.tensor_scalar(digit[:, 1], pos[:], TOPK - 1, None, ALU.bitwise_and))
                for s in range(2):
                    ready()
                    then(nc.vector.tensor_tensor(
                        hit[:], digit[:, s].rearrange("p (n o) -> p n o", o=1).broadcast_to([P, SEL, TOPK]),
                        iota[:, 0:TOPK].rearrange("p (o a) -> p o a", o=1).broadcast_to([P, SEL, TOPK]), ALU.is_equal))
                    ready()
                    h4 = hit[:].rearrange("p (h k) a -> p h k a", h=PH)
                    then(nc.vector.tensor_tensor(h4, h4, x4[:, :, s].rearrange("p h (o a) -> p h o a", o=1).broadcast_to(grid), ALU.mult))
                    ready()
                    then(nc.vector.reduce_sum(sel[:, s], hit[:], AX_X))
                dve.wait_ge(exp_done, tt + 1)
                then(nc.vector.reduce_sum(total[:], best[:], AX_X))
                ready()
                then(nc.vector.reciprocal(total[:], total[:]))
                ready()
                then(nc.vector.tensor_tensor(sel[:, 2].rearrange("p (h k) -> p h k", h=PH), best[:],
                                             total[:].rearrange("p (h o) -> p h o", o=1).broadcast_to([P, PH, TOPK]), ALU.mult))
                dve.wait_ge(t_ready, tt + 1)
                dve.wait_ge(oh_done, GROUPS * tt)
                then(nc.vector.tensor_copy(sel_t[:], ps_t[:, 0:3 * P].rearrange("p (a t) -> p a t", a=3)))
                ready()
                then(nc.vector.tensor_copy(g_hi[:], sel_t[:, 2]))
                ready()
                then(nc.vector.tensor_tensor(g_lo[:], sel_t[:, 2], g_hi[:].bitcast(F32), ALU.subtract))
                hold(dve, step, STEPS * tt + done, passed)
                assert done == STEPS, done
                with dve.Fori(0, GROUPS // 2) as i:
                    for b in range(2):
                        dve.wait_ge(g_ready, GROUPS * tt + 2 * i + b)
                        for j in range(GT):
                            t = bass.ds(2 * GT * i + (GT * b + j), 1)
                            nc.vector.tensor_scalar(one2[:, b, j], iota[:], sel_t[:, 1, t], None, ALU.is_equal)
                            nc.vector.tensor_scalar(one1[:, b, j, 0], iota[:], sel_t[:, 0, t], g_hi[:, t].bitcast(F32), ALU.is_equal, ALU.mult)
                            last = nc.vector.tensor_scalar(one1[:, b, j, 1], iota[:], sel_t[:, 0, t], g_lo[:, t], ALU.is_equal, ALU.mult)
                        last.then_inc(oh_done, 1)

        @block.tensor
        def _(pe):
            pe.wait_ge(consts_in, 32)
            pe.sem_inc(g_ready, 1)
            with pe.Fori(0, TT) as tt:
                pe.wait_ge(step, STEPS * tt + 15)
                for a in range(3):
                    last = nc.tensor.transpose(ps_t[:, a * P:(a + 1) * P], sel[:, a], ident[:])
                last.then_inc(t_ready, 1)
                with pe.Fori(0, GROUPS // 2) as i:
                    for b in range(2):
                        pe.wait_ge(oh_done, GROUPS * tt + 2 * i + b + 1)
                        pe.wait_ge(g_copied, GROUPS * tt + 2 * i + b + 1)
                        for j in range(GT):
                            out = ps_g[:, b, j * NK:(j + 1) * NK]
                            nc.tensor.matmul(out, one2[:, b, j], one1[:, b, j, 0], start=True, stop=False)
                            last = nc.tensor.matmul(out, one2[:, b, j], one1[:, b, j, 1], start=False, stop=True)
                        last.then_inc(g_ready, 1)


def experts(nc, io, keep):
    CHUNKS = NK
    PIECES = 2 * KD
    with ExitStack() as ctx:
        m = Pool(nc, ctx, "e")
        y = m.sb("y", [P, KD, T])
        u_raw = m.sb("u_raw", [P, 2, KD, P])
        u_hi = m.sb("u_hi", [P, 2, KD, P], F32R)
        u_lo = m.sb("u_lo", [P, 2, KD, P], F32R)
        v_raw = m.sb("v_raw", [P, 2, D])
        v_hi = m.sb("v_hi", [P, 4, D], F32R)
        v_lo = m.sb("v_lo", [P, 4, D], F32R)
        g = m.sb("g", [P, 2, T])
        a = m.sb("a", [P, T])
        wa_hi = m.sb("wa_hi", [P, 4, T], F32R)
        wa_lo = m.sb("wa_lo", [P, 4, T], F32R)
        ps_a = m.ps("ps_a", [P, 2, T])
        ps_y = m.ps("ps_y", [P, 4, HALF])
        u_in, v_in, g_in = ([m.sem(f"{x}{b}") for b in range(2)] for x in ("u_in", "v_in", "g_in"))
        u_hi_done, u_lo_done, v_hi_done, v_lo_done, wa_hi_done, wa_lo_done = (m.sem(x) for x in (
            "u_hi_done", "u_lo_done", "v_hi_done", "v_lo_done", "wa_hi_done", "wa_lo_done"))
        a_ready, act_done, gated, y_ready, y_added, x1_in, out_done, stored = (m.sem(x) for x in (
            "a_ready", "act_done", "gated", "y_ready", "y_added", "x1_in", "out_done", "stored"))
        PAIR = PIECES
        block = ctx.enter_context(nc.Block())

        @block.sync
        def _(sp):
            def load(name, c, ring, slot, sems, free):
                sp.wait_ge(free, c + 1)
                dst = ring[:, slot]
                src = io[name][c]
                if name == "u":
                    src = src.rearrange("p (k n) -> p k n", k=KD)
                sp.dma_start(dst, src).then_inc(sems[slot], 16)

            load("u", 0, u_raw, 0, u_in, u_lo_done)
            load("u", 1, u_raw, 1, u_in, u_lo_done)
            with sp.Fori(0, CHUNKS // 2) as p:
                for s in range(2):
                    load("v", 2 * p + s, v_raw, s, v_in, v_lo_done)
                    load("gm_scr", 2 * p + s, g, s, g_in, wa_lo_done)
                    load("u", 2 * p + 2 + s, u_raw, s, u_in, u_lo_done)
            sp.wait_ge(u_in[0], 16 * (CHUNKS // 2 + 1))
            sp.wait_ge(u_in[1], 16 * (CHUNKS // 2 + 1))
            for k in range(KD):
                if k < 2:
                    sp.wait_ge(v_lo_done, CHUNKS + 2)
                else:
                    sp.wait_ge(out_done, k - 1)
                sp.dma_start(v_raw[:, k % 2], io["x1_scr"][k]).then_inc(x1_in, 16)
                if k >= 1:
                    sp.wait_ge(out_done, k)
                    sp.dma_start(io["out"][:, (k - 1) * T:k * T], y[:, k - 1]).then_inc(stored, 16)
                sp.wait_ge(x1_in, 16 * (k + 1))
            sp.wait_ge(out_done, KD)
            sp.dma_start(io["out"][:, (KD - 1) * T:KD * T], y[:, KD - 1]).then_inc(stored, 16)
            sp.wait_ge(stored, 16 * KD)

        @block.scalar
        def _(act):
            def split_u(c, s):
                act.wait_ge(u_in[s], 16 * (c // 2 + 1) if isinstance(c, int) else 16 * c[0] + 16)
                c = c if isinstance(c, int) else 2 * c[0] + c[1]
                act.wait_ge(a_ready, c + 1)
                nc.scalar.activation(u_hi[:, s], u_raw[:, s], ACT.Copy).then_inc(u_hi_done, 1)

            def activate(p, s, r):
                c = 2 * p + s
                act.wait_ge(a_ready, c + 3)
                act.wait_ge(gated, c)
                nc.scalar.activation(a[:], ps_a[:, s], ACT.Gelu_apprx_tanh).then_inc(act_done, 1)
                act.wait_ge(gated, c + 1)
                nc.scalar.activation(wa_hi[:, r], g[:, s], ACT.Copy).then_inc(wa_hi_done, 1)

            act.sem_inc(act_done, 2)
            split_u(0, 0)
            split_u(1, 1)
            with act.Fori(0, CHUNKS // 4) as i:
                for h in range(2):
                    p = 2 * i + h
                    act.wait_ge(y_ready, PAIR * p + PAIR)
                    for s in range(2):
                        act.wait_ge(v_in[s], 16 * p + 16)
                        nc.scalar.activation(v_hi[:, 2 * h + s], v_raw[:, s], ACT.Copy).then_inc(v_hi_done, 1)
                    split_u((p + 1, 0), 0)
                    activate(p, 0, 2 * h)
                    activate(p, 1, 2 * h + 1)
                    split_u((p + 1, 1), 1)

        @block.vector
        def _(dve):
            def lo(dst, raw, hi, hi_done, count, done):
                dve.wait_ge(hi_done, count)
                nc.vector.tensor_tensor(dst, raw, hi.bitcast(F32), ALU.subtract).then_inc(done, 1)

            def step(p, h, add):
                for s in range(2):
                    lo(v_lo[:, 2 * h + s], v_raw[:, s], v_hi[:, 2 * h + s], v_hi_done, 2 * p + s + 1, v_lo_done)
                lo(u_lo[:, 0], u_raw[:, 0], u_hi[:, 0], u_hi_done, 2 * p + 3, u_lo_done)
                for s in range(2):
                    c = 2 * p + s
                    dve.wait_ge(g_in[s], 16 * p + 16)
                    dve.wait_ge(act_done, c + 3)
                    nc.vector.tensor_tensor(g[:, s], g[:, s], a[:], ALU.mult).then_inc(gated, 1)
                    lo(wa_lo[:, 2 * h + s], g[:, s], wa_hi[:, 2 * h + s], wa_hi_done, c + 1, wa_lo_done)
                lo(u_lo[:, 1], u_raw[:, 1], u_hi[:, 1], u_hi_done, 2 * p + 4, u_lo_done)
                if add:
                    add_pair(p - 1)

            def add_pair(p):
                dve.wait_ge(y_added, PAIR * p + 4)
                for j in range(PIECES):
                    out = y[:, j // 2, (j % 2) * HALF:(j % 2 + 1) * HALF]
                    dve.wait_ge(y_ready, PAIR * p + (2 * PAIR + j + 1))
                    nc.vector.tensor_tensor(out, out, ps_y[:, j % 4], ALU.add).then_inc(y_added, 1)

            for sem in (u_lo_done, v_lo_done, wa_lo_done):
                dve.sem_inc(sem, 2)
            nc.vector.memset(y[:], 0.0).then_inc(y_added, 4)
            for s in range(2):
                lo(u_lo[:, s], u_raw[:, s], u_hi[:, s], u_hi_done, s + 1, u_lo_done)
            step(0, 0, False)
            step(1, 1, True)
            with dve.Fori(1, CHUNKS // 4) as i:
                for h in range(2):
                    step(2 * i + h, h, True)
            add_pair(CHUNKS // 2 - 1)
            dve.wait_ge(y_added, PAIR * CHUNKS // 2 + 4)
            for k in range(KD):
                dve.wait_ge(x1_in, 16 * (k + 1))
                nc.vector.scalar_tensor_tensor(out=y[:, k], in0=y[:, k], scalar=keep.mod[:, 5 * KD + k:5 * KD + k + 1], in1=v_raw[:, k % 2],
                                               op0=ALU.mult, op1=ALU.add).then_inc(out_done, 1)

        @block.tensor
        def _(pe):
            def activations(p):
                for s in range(2):
                    c = 2 * p + s
                    pe.wait_ge(u_lo_done, c + 3)
                    pe.wait_ge(act_done, c + 1)
                    for k in range(KD):
                        for c0, c1 in split_columns(T):
                            last = product3(nc, ps_a[:, s, c0:c1], u_hi[:, s, k], u_lo[:, s, k], keep.h2_hi[:, k, c0:c1], keep.h2_lo[:, k, c0:c1],
                                            k == 0, k == KD - 1)
                    last.then_inc(a_ready, 1)

            def outputs(p, h):
                pe.wait_ge(wa_lo_done, 2 * p + 4)
                pe.wait_ge(v_lo_done, 2 * p + 4)
                for j in range(PIECES):
                    d, c0 = j // 2, (j % 2) * HALF
                    pe.wait_ge(y_added, PAIR * p + (j + 1))
                    for s in range(2):
                        r = 2 * h + s
                        last = product3(nc, ps_y[:, j % 4], v_hi[:, r, d * P:(d + 1) * P], v_lo[:, r, d * P:(d + 1) * P],
                                        wa_hi[:, r, c0:c0 + HALF], wa_lo[:, r, c0:c0 + HALF], s == 0, s == 1)
                    last.then_inc(y_ready, 1)

            pe.sem_inc(a_ready, 2)
            pe.sem_inc(y_ready, 2 * PAIR)
            activations(0)
            activations(1)
            outputs(0, 0)
            with pe.Fori(1, CHUNKS // 4) as i:
                for h in range(2):
                    activations(2 * i + h)
                    outputs(2 * i + h - 1, 1 - h)
            outputs(CHUNKS // 2 - 1, 1)


class Keep:
    pass


def build(nc, io, upto=99):
    with ExitStack() as ctx:
        keep = Keep()
        m = Pool(nc, ctx, "keep")
        keep.norm_w = m.sb("norm_w", [P, 2 * KD])
        keep.mod = m.sb("mod", [P, 6 * KD])
        keep.mod_c = m.sb("mod_c", [P, 2 * KD])
        keep.gain = m.sb("gain", [P, 3, KD])
        with ExitStack() as front:
            f = Pool(nc, front, "front")
            context = front.enter_context(ExitStack())
            fc = Pool(nc, context, "front_ctx")
            lat = [f.sb(x, [P, KD, T], F32R) for x in ("h_hi", "h_lo")]
            con = [fc.sb(x, [P, KD, C], F32R) for x in ("h_hi", "h_lo")]
            keep.h_hi, keep.h_lo = Columns(lat[0], con[0]), Columns(lat[1], con[1])
            adaln_and_norm1(nc, io, keep)
            if upto < 1:
                return
            for name, shape in (("v", (TC, HEADS * HD)), ("oa", (PAIRS, P, T)), ("ob", (BLOCKS, P, T)), ("mg", (KD, P, T)), ("x1", (KD, P, T)),
                                ("gm", (NK, P, T))):
                io[name + "_scr"] = nc.dram_tensor(name + "_scratch", shape, F32, kind="Internal").ap()
            values(nc, io, keep)
            attention(nc, io, keep)
            if upto < 2:
                return
            recurrence(nc, io, keep)
            context.close()
            if upto < 3:
                return
            merge(nc, io, keep)
        b = Pool(nc, ctx, "back")
        keep.h2_hi = b.sb("h2_hi", [P, KD, T], F32R)
        keep.h2_lo = b.sb("h2_lo", [P, KD, T], F32R)
        project(nc, io, keep)
        if upto < 4:
            return
        with ExitStack() as chosen:
            c = Pool(nc, chosen, "chosen")
            keep.best = c.sb("best", [P, TT, 2 * PH, TOPK])
            keep.place = c.sb("place", [P, TT, 2 * PH, TOPK])
            route(nc, io, keep)
            if upto < 5:
                return
            gates(nc, io, keep)
        if upto < 6:
            return
        experts(nc, io, keep)


IN_SHAPES = {
    "xt": (P, KD * T), "ctxt": (P, KD * C), "cc": (P, KD * 2), "w_ada": (12, P, KD * 512), "b_ada": (P, 6 * KD),
    "norm_w": (P, 2 * KD), "w_v": (P, KD * 512), "w_q": (PAIRS, P, KD * P), "w_k": (PAIRS, P, KD * P), "qk_w": (P, 2), "mask": (P, GRID_W),
    "ident": (P, P), "head_ones": (P, P), "rpb": (PAIRS, P, DR * GRID_W),
    "w_xr": (BLOCKS + 1, P, KD * P), "w_yr": (BLOCKS + 1, P, KD * P), "lru_vec": (P, BLOCKS * NVEC), "w_gates": (BLOCKS, P, 4 * P),
    "w_ga": (KD, P, KD * P), "w_gb": (KD, P, KD * P), "w_oa": (KD, P, PAIRS * P), "w_ol": (KD, P, KD * P), "w_out": (KD, P, KD * P),
    "w_pq": (2 * PH + 1, P, KD * P), "keys": (P, 2 * PH * NK), "iota": (P, NK), "u": (NK + 2, P, KD * P), "v": (NK, P, D),
}


def by_partition(v):
    return np.ascontiguousarray(v.reshape(-1, P).T)


def chunks(w, n):
    k, cols = w.shape
    return np.ascontiguousarray(w.reshape(k // P, P, cols // n, n).transpose(2, 1, 0, 3)).reshape(cols // n, P, -1)


def layout(inp):
    a = {k: np.asarray(v) for k, v in inp.items()}
    out = {}
    rows = lambda v: np.ascontiguousarray(v.T.reshape(KD, P, -1).transpose(1, 0, 2)).reshape(P, -1)
    out["xt"] = rows(a["x"][0])
    out["ctxt"] = rows(a["ctx"][0])
    out["cc"] = rows(np.concatenate([a["c"], a["c_ctx"][None]], axis=0))
    out["w_ada"] = chunks(a["w_ada"][0], 512)
    out["b_ada"] = by_partition(a["b_ada"][0])
    out["norm_w"] = by_partition(np.concatenate([a["norm1_w"][0], a["norm2_w"][0]]))
    w_in = a["w_in"][0]
    na = HEADS * HD
    out["w_q"] = chunks(w_in[:, 0:na], P)
    out["w_k"] = chunks(w_in[:, na:2 * na], P)
    out["w_v"] = chunks(w_in[:, 2 * na:3 * na], na)[0]
    out["qk_w"] = np.stack([np.tile(a["q_norm_w"][0], 2), np.tile(a["k_norm_w"][0], 2)], axis=1)
    xr0 = 3 * na
    again = lambda w: np.concatenate([w, w[:1]])
    out["w_xr"] = again(chunks(w_in[:, xr0:xr0 + D], P))
    out["w_yr"] = again(chunks(w_in[:, xr0 + D:xr0 + 2 * D], P))
    out["w_ga"] = chunks(w_in[:, xr0 + 2 * D:xr0 + 3 * D], P)
    out["w_gb"] = chunks(w_in[:, xr0 + 3 * D:], P)
    out["w_oa"], out["w_ol"], out["w_out"] = (chunks(a[n][0], P) for n in ("w_o_attn", "w_o_lru", "w_out"))
    out["w_pq"] = again(chunks(a["peer_w_q"][0], P))
    out["keys"] = np.ascontiguousarray(a["peer_keys"][0].transpose(3, 0, 1, 2)).reshape(P, -1)
    out["iota"] = np.tile(np.arange(NK, dtype=np.float32), (P, 1))
    u = a["peer_u"][0].reshape(NK, NK, KD, P).transpose(0, 3, 2, 1).reshape(NK, P, KD * P)
    out["u"] = np.concatenate([u, u[:2]])
    out["v"] = a["peer_v"][0].reshape(NK, NK, D)
    bias4 = np.stack([a["lru_b_a"][0, 0], a["lru_b_x"][0, 0], a["lru_b_a"][0, 1], a["lru_b_x"][0, 1]])
    vec = np.concatenate([a["conv_w"][0], a["conv_b"], bias4, a["lru_lambda"][0]])
    out["lru_vec"] = np.ascontiguousarray(vec.reshape(NVEC, BLOCKS, P).transpose(2, 1, 0)).reshape(P, -1)
    gates = np.stack([a["lru_w_a"][0, 0], a["lru_w_x"][0, 0], a["lru_w_a"][0, 1], a["lru_w_x"][0, 1]], axis=2)
    out["w_gates"] = gates.reshape(BLOCKS, P, 4 * P)
    rpb = a["na_rpb"][0]
    mask = np.full((GRID_W, GRID_W), NEG, np.float32)
    bias = np.zeros((HEADS, GRID_W, DR, GRID_W), np.float32)
    for c in range(GRID_W):
        lo = min(max(c - WIN_COLS // 2, 0), GRID_W - WIN_COLS)
        mask[c, lo:lo + WIN_COLS] = 0.0
        first = lo - c + WIN_COLS - 1
        bias[:, c, :, lo:lo + WIN_COLS] = rpb[:, :, first:first + WIN_COLS]
    out["mask"] = np.tile(mask, (2, 1))
    out["rpb"] = bias.reshape(PAIRS, P, DR * GRID_W)
    out["ident"] = np.eye(P, dtype=np.float32)
    out["head_ones"] = np.kron(np.eye(2, dtype=np.float32), np.ones((HD, HD), np.float32))
    return out


def kernel(**inputs):
    import concourse.bacc as bacc
    from concourse.bass_utils import run_bass_kernel_spmd

    arrays = layout(inputs)
    nc = bacc.Bacc("TRN2", target_bir_lowering=False, num_devices=1)
    io = {name: nc.dram_tensor("in_" + name, shape, F32, kind="ExternalInput").ap() for name, shape in IN_SHAPES.items()}
    io["out"] = nc.dram_tensor("out", (P, KD * T), F32, kind="ExternalOutput").ap()
    build(nc, io)
    r = run_bass_kernel_spmd(nc, [{"in_" + name: arrays[name] for name in IN_SHAPES}], core_ids=[0])
    y = np.asarray(r.results[0]["out"]).reshape(P, KD, T)
    return np.ascontiguousarray(y.transpose(2, 1, 0)).reshape(1, T, D)
```

```python
from contextlib import ExitStack

import numpy as np

import concourse.bass as bass
from concourse import mybir

F32 = mybir.dt.float32
F32R = mybir.dt.float32r
BF16 = mybir.dt.bfloat16
U32 = mybir.dt.uint32
ALU = mybir.AluOpType
ACT = mybir.ActivationFunctionType
AX_X = mybir.AxisListType.X

P = 128
D = 1024
KD = D // P
T = 1024
C = 256
TC = T + C
HALF = 512
EPS = 1e-6
NEG = -1e30

HEADS = 8
HD = 64
PAIRS = HEADS // 2
GRID_W = 64
ROWS = T // GRID_W
WIN = 8
WIN_COLS = 16
DR = 2 * WIN - 1
SCALE = HD ** -0.5
VT = TC // P
VS = T // P - 1

BLOCKS = 8
CONV = 4
CONV_LEFT = 2

NK = 128
TOPK = 16
PH = 8
TT = T // P
NEXP = NK * NK


def split_columns(n):
    return [(a, min(n, a + HALF)) for a in range(0, n, HALF)]


def product3(nc, out, w_hi, w_lo, x_hi, x_lo, first, last):
    nc.tensor.matmul(out, w_hi, x_hi, start=first, stop=False)
    nc.tensor.matmul(out, w_hi, x_lo, start=False, stop=False)
    return nc.tensor.matmul(out, w_lo, x_hi, start=False, stop=last)


class Columns:

    def __init__(self, lat, con):
        self.lat, self.con = lat, con

    def at(self, k, a, b):
        return self.lat[:, k, a:b] if b <= T else self.con[:, k, a - T:b - T]


class Pool:

    def __init__(self, nc, ctx, prefix):
        self.nc, self.ctx, self.prefix = nc, ctx, prefix

    def sb(self, name, shape, dt=F32):
        return self.ctx.enter_context(self.nc.sbuf_tensor(f"{self.prefix}_{name}", shape, dt))

    def ps(self, name, shape):
        return self.ctx.enter_context(self.nc.psum_tensor(f"{self.prefix}_{name}", shape, F32))

    def sem(self, name):
        return self.ctx.enter_context(self.nc.semaphore(f"{self.prefix}_{name}"))

    def cleared_sem(self, name, cleared):
        handle = self.nc.alloc_semaphore(name=f"{self.prefix}_{name}")
        cleared.append(handle)
        return handle


def adaln_and_norm1(nc, io, keep):
    PIECE = 256
    RING = 4
    FIRST = 2 * D // PIECE
    PIECES = 6 * D // PIECE
    GROUPS = PIECE // P
    sems = []
    with ExitStack() as ctx:
        m = Pool(nc, ctx, "a")
        xt = m.sb("xt", [P, KD, TC])
        w = m.sb("w", [P, RING, KD, PIECE])
        cc = m.sb("cc", [P, KD, 2])
        silu_c = m.sb("silu_c", [P, KD, 2])
        b_ada = m.sb("b_ada", [P, 6 * KD])
        ones = m.sb("ones", [P, P])
        eps = m.sb("eps", [P, 1])
        sq = m.sb("sq", [P, 2, TC])
        root = m.sb("root", [P, TC])
        rstd = m.sb("rstd", [P, TC])
        p1 = m.sb("p1", [P, 3, KD])
        hn = m.sb("hn", [P, 2, TC])
        hm = m.sb("hm", [P, 2, TC])
        ps_sum = m.ps("ps_sum", [P, 3 * HALF])
        ps_first = m.ps("ps_first", [P, HALF])
        ps_rest = m.ps("ps_rest", [P, HALF])
        (x_in, small_in, w_used, silu_done, sq_done, sq_used, consts, root_done, vec, normed, modulated, hi_done, lo_done) = (
            m.cleared_sem(x, sems) for x in ("x_in", "small_in", "w_used", "silu_done", "sq_done", "sq_used", "consts", "root_done",
                                             "vec", "normed", "modulated", "hi_done", "lo_done"))
        w_in = [m.cleared_sem(f"w_in{b}", sems) for b in range(RING)]
        block = ctx.enter_context(nc.Block())

        @block.sync
        def _(sp):
            sp.dma_start(cc[:], io["cc"].rearrange("p (k v) -> p k v", v=2)).then_inc(small_in, 16)
            sp.dma_start(b_ada[:], io["b_ada"]).then_inc(small_in, 16)
            sp.dma_start(keep.norm_w[:], io["norm_w"]).then_inc(small_in, 16)
            sp.dma_start(xt[:, :, 0:T], io["xt"].rearrange("p (k t) -> p k t", k=KD)).then_inc(x_in, 16)
            sp.dma_start(xt[:, :, T:TC], io["ctxt"].rearrange("p (k t) -> p k t", k=KD)).then_inc(x_in, 16)
            with sp.Fori(0, PIECES // RING) as i:
                for b in range(RING):
                    sp.wait_ge(w_used, RING * i + b + 1)
                    sp.dma_start(w[:, b], io["w_ada"][RING * i + b].rearrange("p (k n) -> p k n", k=KD)).then_inc(w_in[b], 16)

        @block.scalar
        def _(act):
            act.wait_ge(small_in, 48)
            nc.scalar.activation(silu_c[:], cc[:], ACT.Silu).then_inc(silu_done, 1)
            act.wait_ge(x_in, 32)
            for k in range(KD):
                if k >= 2:
                    act.wait_ge(sq_used, k - 1)
                nc.scalar.activation(sq[:, k % 2], xt[:, k], ACT.Square).then_inc(sq_done, 1)
            act.wait_ge(sq_used, KD)
            act.wait_ge(consts, 2)
            nc.scalar.activation(root[:], ps_sum[:, 0:TC], ACT.Sqrt, bias=eps[:], scale=1.0 / D).then_inc(root_done, 1)
            for k in range(KD):
                act.wait_ge(modulated, 2 * k + 2)
                for a, b in ((0, T), (T, TC)):
                    nc.scalar.activation(keep.h_hi.at(k, a, b), hm[:, k % 2, a:b], ACT.Copy).then_inc(hi_done, 1)

        @block.tensor
        def _(pe):
            pe.wait_ge(consts, 2)
            for k in range(KD):
                pe.wait_ge(sq_done, k + 1)
                for a, b in split_columns(TC):
                    last = nc.tensor.matmul(ps_sum[:, a:b], ones[:], sq[:, k % 2, a:b], start=(k == 0), stop=(k == KD - 1))
                last.then_inc(sq_used, 1)
            pe.wait_ge(silu_done, 1)
            pe.sem_inc(w_used, RING)
            for first, end, ps_mod in ((0, FIRST, ps_first), (FIRST, PIECES, ps_rest)):
                with pe.Fori(first // RING, end // RING) as i:
                    for b in range(RING):
                        pe.wait_ge(w_in[b], 16 * (i + 1))
                        for g in range(GROUPS):
                            col = (RING * i + b - first) * 2 * GROUPS + 2 * g
                            for k in range(KD):
                                last = nc.tensor.matmul(ps_mod[:, bass.ds(col, 2)], w[:, b, k, g * P:(g + 1) * P], silu_c[:, k, :],
                                                        start=(k == 0), stop=(k == KD - 1))
                        last.then_inc(w_used, 1)

        @block.vector
        def _(dve):
            nc.vector.memset(ones[:], 1.0).then_inc(consts, 1)
            nc.vector.memset(eps[:], EPS).then_inc(consts, 1)
            dve.wait_ge(root_done, 1)
            nc.vector.reciprocal(rstd[:], root[:]).then_inc(vec, 1)
            dve.wait_ge(w_used, RING + FIRST)
            dve.wait_ge(small_in, 48)
            pm = ps_first[:, 0:4 * KD].rearrange("p (n v) -> p n v", v=2)
            nc.vector.tensor_tensor(keep.mod[:, 0:2 * KD], pm[:, :, 0], b_ada[:, 0:2 * KD], ALU.add).then_inc(vec, 1)
            nc.vector.tensor_tensor(keep.mod_c[:], pm[:, :, 1], b_ada[:, 0:2 * KD], ALU.add).then_inc(vec, 1)
            dve.wait_ge(vec, 3)
            nc.vector.tensor_scalar_add(p1[:, 0], keep.mod[:, KD:2 * KD], 1.0).then_inc(vec, 1)
            nc.vector.tensor_scalar_add(p1[:, 1], keep.mod_c[:, KD:2 * KD], 1.0).then_inc(vec, 1)
            dve.wait_ge(vec, 5)
            nc.vector.tensor_tensor(keep.gain[:, 0], p1[:, 0], keep.norm_w[:, 0:KD], ALU.mult).then_inc(vec, 1)
            nc.vector.tensor_tensor(keep.gain[:, 1], p1[:, 1], keep.norm_w[:, 0:KD], ALU.mult).then_inc(vec, 1)
            dve.wait_ge(vec, 7)
            for k in range(KD):
                nc.vector.tensor_tensor(hn[:, k % 2], xt[:, k], rstd[:], ALU.mult).then_inc(normed, 1)
                dve.wait_ge(normed, k + 1)
                nc.vector.tensor_scalar(hm[:, k % 2, 0:T], hn[:, k % 2, 0:T], keep.gain[:, 0, k:k + 1], keep.mod[:, k:k + 1],
                                        ALU.mult, ALU.add).then_inc(modulated, 1)
                nc.vector.tensor_scalar(hm[:, k % 2, T:TC], hn[:, k % 2, T:TC], keep.gain[:, 1, k:k + 1], keep.mod_c[:, k:k + 1],
                                        ALU.mult, ALU.add).then_inc(modulated, 1)
                dve.wait_ge(hi_done, 2 * k + 2)
                for a, b in ((0, T), (T, TC)):
                    nc.vector.tensor_tensor(keep.h_lo.at(k, a, b), hm[:, k % 2, a:b], keep.h_hi.at(k, a, b).bitcast(F32), ALU.subtract)\
                        .then_inc(lo_done, 1)
                dve.wait_ge(lo_done, 2 * k + 2)
            dve.wait_ge(w_used, RING + PIECES)
            rest = ps_rest[:, 0:8 * KD].rearrange("p (n v) -> p n v", v=2)
            nc.vector.tensor_tensor(keep.mod[:, 2 * KD:6 * KD], rest[:, :, 0], b_ada[:, 2 * KD:6 * KD], ALU.add).then_inc(vec, 1)
            dve.wait_ge(vec, 8)
            nc.vector.tensor_scalar_add(p1[:, 2], keep.mod[:, 4 * KD:5 * KD], 1.0).then_inc(vec, 1)
            dve.wait_ge(vec, 9)
            nc.vector.tensor_tensor(keep.gain[:, 2], p1[:, 2], keep.norm_w[:, KD:2 * KD], ALU.mult).then_inc(vec, 1)
    nc.clear_and_free_semaphores(sems)
    nc.all_engine_barrier()


def values(nc, io, keep):
    W = HEADS * HD
    with ExitStack() as ctx:
        m = Pool(nc, ctx, "v")
        raw = m.sb("raw", [P, KD, W])
        w_hi = m.sb("w_hi", [P, KD, W], F32R)
        w_lo = m.sb("w_lo", [P, KD, W], F32R)
        v = m.sb("v", [P, 2, W])
        acc = m.ps("acc", [P, 2, W])
        w_in, hi_done, lo_done, acc_ready, v_ready = m.sem("w_in"), m.sem("hi_done"), m.sem("lo_done"), m.sem("acc_ready"), m.sem("v_ready")
        stored = [m.sem(f"stored{b}") for b in range(2)]
        block = ctx.enter_context(nc.Block())

        @block.sync
        def _(sp):
            sp.dma_start(raw[:], io["w_v"].rearrange("p (k n) -> p k n", k=KD)).then_inc(w_in, 16)
            for j in range(VT):
                sp.wait_ge(v_ready, j + 1)
                sp.dma_start(io["v_scr"][j * P:(j + 1) * P, :], v[:, j % 2]).then_inc(stored[j % 2], 16)
            for b in range(2):
                sp.wait_ge(stored[b], 16 * (VT // 2))

        @block.scalar
        def _(act):
            act.wait_ge(w_in, 16)
            for k in range(KD):
                nc.scalar.activation(w_hi[:, k], raw[:, k], ACT.Copy).then_inc(hi_done, 1)
            for j in range(VT):
                act.wait_ge(acc_ready, j + 1)
                if j >= 2:
                    act.wait_ge(stored[j % 2], 16 * (j // 2))
                nc.scalar.activation(v[:, j % 2], acc[:, j % 2], ACT.Copy).then_inc(v_ready, 1)

        @block.vector
        def _(dve):
            for k in range(KD):
                dve.wait_ge(hi_done, k + 1)
                nc.vector.tensor_tensor(w_lo[:, k], raw[:, k], w_hi[:, k].bitcast(F32), ALU.subtract).then_inc(lo_done, 1)

        @block.tensor
        def _(pe):
            for j in range(VT):
                if j >= 2:
                    pe.wait_ge(v_ready, j - 1)
                tile = (j * P, (j + 1) * P)
                for k in range(KD):
                    pe.wait_ge(lo_done, k + 1)
                    out = acc[:, j % 2]
                    nc.tensor.matmul(out, keep.h_hi.at(k, *tile), w_hi[:, k], start=(k == 0), stop=False)
                    nc.tensor.matmul(out, keep.h_hi.at(k, *tile), w_lo[:, k], start=False, stop=False)
                    last = nc.tensor.matmul(out, keep.h_lo.at(k, *tile), w_hi[:, k], start=False, stop=(k == KD - 1))
                last.then_inc(acc_ready, 1)


def attention(nc, io, keep):
    KEYS = WIN * GRID_W
    ALL = KEYS + C
    NT = ALL // P
    row0 = [min(max(r - WIN // 2, 0), ROWS - WIN) for r in range(ROWS)]
    with ExitStack() as ctx:
        m = Pool(nc, ctx, "at")
        raw = m.sb("raw", [P, 2, KD, P])
        w_hi = m.sb("w_hi", [P, 2, KD, P], F32R)
        w_lo = m.sb("w_lo", [P, 2, KD, P], F32R)
        qk_w = m.sb("qk_w", [P, 2])
        q_w = m.sb("q_w", [P, 1])
        head_ones = m.sb("head_ones", [P, P])
        ident = m.sb("ident", [P, P])
        eps = m.sb("eps", [P, 1])
        mask = m.sb("mask", [P, GRID_W])
        slab = m.sb("slab", [P, DR, GRID_W])
        sq = m.sb("sq", [P, TC])
        root = m.sb("root", [P, TC])
        rstd = m.sb("rstd", [P, TC])
        q = m.sb("q", [P, ROWS, P])
        k_t = m.sb("k_t", [P, TC])
        v = m.sb("v", [P, VT, P])
        v_odd = m.sb("v_odd", [P, VS, P])
        s = m.sb("s", [P, 2, KEYS])
        p = m.sb("p", [P, 2, ALL])
        p_t = m.sb("p_t", [P, 2, NT, P])
        stat = m.sb("stat", [P, 2, 8])
        o = m.sb("o", [P, T])
        ps_a = m.ps("ps_a", [P, 3 * HALF])
        ps_b = m.ps("ps_b", [P, 3 * HALF])
        ps_t = m.ps("ps_t", [P, 2 * HALF])
        score = [ps_a, ps_b]
        consts_in, q_in, k_in, slab_in, v_in = (m.sem(x) for x in ("consts_in", "q_in", "k_in", "slab_in", "v_in"))
        hi_done, lo_done, proj_done, sq_done, sum_done, root_done = (m.sem(x) for x in (
            "hi_done", "lo_done", "proj_done", "sq_done", "sum_done", "root_done"))
        consts, rstd_done, q_done, k_done, slab_done = (m.sem(x) for x in ("consts", "rstd_done", "q_done", "k_done", "slab_done"))
        s_ready, row_max, row_stat, exp_done, p_norm, p_ready = (m.sem(x) for x in (
            "s_ready", "row_max", "row_stat", "exp_done", "p_norm", "p_ready"))
        t_ready, t_copied, o_ready, o_copied, o_stored = (m.sem(x) for x in ("t_ready", "t_copied", "o_ready", "o_copied", "o_stored"))
        block = ctx.enter_context(nc.Block())

        @block.sync
        def _(sp):
            sp.dma_start(qk_w[:], io["qk_w"]).then_inc(consts_in, 16)
            sp.dma_start(mask[:], io["mask"]).then_inc(consts_in, 16)
            sp.dma_start(ident[:], io["ident"]).then_inc(consts_in, 16)
            sp.dma_start(head_ones[:], io["head_ones"]).then_inc(consts_in, 16)
            with sp.Fori(0, PAIRS) as h:
                v_col = sp.snap(h * P)
                sp.wait_ge(lo_done, 2 * h)
                sp.dma_start(raw[:, 0], io["w_q"][h].rearrange("p (k n) -> p k n", k=KD)).then_inc(q_in, 16)
                sp.dma_start(raw[:, 1], io["w_k"][h].rearrange("p (k n) -> p k n", k=KD)).then_inc(k_in, 16)
                sp.wait_ge(row_max, ROWS * h)
                sp.dma_start(slab[:], io["rpb"][h].rearrange("p (d c) -> p d c", d=DR)).then_inc(slab_in, 16)
                sp.wait_ge(o_ready, ROWS * h)
                sp.dma_start(v[:], io["v_scr"][:, bass.ds(v_col, P)].rearrange("(j p) c -> p j c", p=P)).then_inc(v_in, 16)
                sp.dma_start(v_odd[:], io["v_scr"][GRID_W:GRID_W + VS * P, bass.ds(v_col, P)].rearrange("(j p) c -> p j c", p=P))\
                    .then_inc(v_in, 16)
                sp.wait_ge(o_copied, ROWS * (h + 1))
                sp.dma_start(io["oa_scr"][h], o[:]).then_inc(o_stored, 16)
            sp.wait_ge(o_stored, 16 * PAIRS)

        @block.scalar
        def _(act):
            act.wait_ge(consts, 1)
            with act.Fori(0, PAIRS) as h:
                act.wait_ge(q_in, 16 * (h + 1))
                nc.scalar.activation(w_hi[:, 0], raw[:, 0], ACT.Copy).then_inc(hi_done, 1)
                act.wait_ge(k_in, 16 * (h + 1))
                nc.scalar.activation(w_hi[:, 1], raw[:, 1], ACT.Copy).then_inc(hi_done, 1)
                act.wait_ge(proj_done, 2 * h + 1)
                nc.scalar.activation(sq[:, 0:T], ps_a[:, 0:T], ACT.Square).then_inc(sq_done, 1)
                act.wait_ge(sum_done, 2 * h + 1)
                nc.scalar.activation(root[:, 0:T], ps_t[:], ACT.Sqrt, bias=eps[:], scale=1.0 / HD).then_inc(root_done, 1)
                act.wait_ge(proj_done, 2 * h + 2)
                nc.scalar.activation(sq[:], ps_b[:, 0:TC], ACT.Square).then_inc(sq_done, 1)
                act.wait_ge(sum_done, 2 * h + 2)
                act.wait_ge(rstd_done, 2 * h + 1)
                nc.scalar.activation(root[:], ps_a[:, 0:TC], ACT.Sqrt, bias=eps[:], scale=1.0 / HD).then_inc(root_done, 1)
                for i in range(ROWS + 2):
                    if i < ROWS:
                        g, b = ROWS * h + i, i % 2
                        act.wait_ge(row_max, g + 1)
                        if i >= 2:
                            act.wait_ge(t_ready, g - 1)
                        nc.scalar.activation(p[:, b, 0:KEYS], s[:, b], ACT.Exp, bias=stat[:, b, 2:3], accum_out=stat[:, b, 3:4])
                        nc.scalar.activation(p[:, b, KEYS:ALL], score[b][:, KEYS:ALL], ACT.Exp, bias=stat[:, b, 2:3],
                                             accum_out=stat[:, b, 4:5]).then_inc(exp_done, 1)
                    if i >= 2:
                        r = i - 2
                        act.wait_ge(t_ready, ROWS * h + r + 1)
                        if r >= 2:
                            act.wait_ge(o_ready, ROWS * h + r - 1)
                        nc.scalar.activation(p_t[:, r % 2], ps_t[:, 0:ALL].rearrange("p (j n) -> p j n", j=NT), ACT.Copy)\
                            .then_inc(t_copied, 1)

        @block.vector
        def _(dve):
            nc.vector.memset(eps[:], EPS).then_inc(consts, 1)
            nc.vector.memset(q[:], 0.0).then_inc(consts, 1)
            dve.wait_ge(consts_in, 64)
            nc.vector.tensor_scalar_mul(q_w[:], qk_w[:, 0:1], SCALE).then_inc(consts, 1)
            dve.wait_ge(consts, 3)
            with dve.Fori(0, PAIRS) as h:
                for u in range(2):
                    dve.wait_ge(hi_done, 2 * h + u + 1)
                    nc.vector.tensor_tensor(w_lo[:, u], raw[:, u], w_hi[:, u].bitcast(F32), ALU.subtract).then_inc(lo_done, 1)
                dve.wait_ge(slab_in, 16 * (h + 1))
                nc.vector.tensor_tensor(slab[:], slab[:], mask[:].rearrange("p (a c) -> p a c", a=1).broadcast_to([P, DR, GRID_W]), ALU.add)\
                    .then_inc(slab_done, 1)
                dve.wait_ge(root_done, 2 * h + 1)
                nc.vector.reciprocal(rstd[:, 0:T], root[:, 0:T]).then_inc(rstd_done, 1)
                dve.wait_ge(rstd_done, 2 * h + 1)
                for a in range(2):
                    half = slice(a * HD, (a + 1) * HD)
                    nc.vector.scalar_tensor_tensor(
                        out=q[half, :, half], in0=ps_a[half, 0:T].rearrange("p (r c) -> p r c", r=ROWS), scalar=q_w[half],
                        in1=rstd[half, 0:T].rearrange("p (r c) -> p r c", r=ROWS), op0=ALU.mult, op1=ALU.mult).then_inc(q_done, 1)
                dve.wait_ge(root_done, 2 * h + 2)
                dve.wait_ge(q_done, 2 * h + 2)
                nc.vector.reciprocal(rstd[:], root[:]).then_inc(rstd_done, 1)
                dve.wait_ge(rstd_done, 2 * h + 2)
                nc.vector.scalar_tensor_tensor(out=k_t[:], in0=ps_b[:, 0:TC], scalar=qk_w[:, 1:2], in1=rstd[:],
                                               op0=ALU.mult, op1=ALU.mult).then_inc(k_done, 1)
                dve.wait_ge(slab_done, h + 1)
                dve.wait_ge(o_stored, 16 * h)
                for i in range(ROWS + 3):
                    if i < ROWS:
                        g, b = ROWS * h + i, i % 2
                        dve.wait_ge(s_ready, g + 1)
                        if i >= 2:
                            dve.wait_ge(exp_done, g - 1)
                            dve.wait_ge(p_ready, g - 1)
                        d0 = row0[i] - i + WIN - 1
                        nc.vector.reduce_max(stat[:, b, 1:2], score[b][:, KEYS:ALL], AX_X).then_inc(row_stat, 1)
                        nc.vector.tensor_tensor_reduce(
                            out=s[:, b], in0=score[b][:, 0:KEYS], in1=slab[:, d0:d0 + WIN].rearrange("p d c -> p (d c)"), scale=1.0,
                            scalar=-3e38, op0=ALU.add, op1=ALU.max, accum_out=stat[:, b, 0:1]).then_inc(row_stat, 1)
                        dve.wait_ge(row_stat, 2 * g + 2)
                        nc.vector.tensor_scalar(stat[:, b, 2:3], stat[:, b, 0:1], stat[:, b, 1:2], -1.0, ALU.max, ALU.mult)\
                            .then_inc(row_max, 1)
                    if 1 <= i <= ROWS:
                        r = i - 1
                        g, b = ROWS * h + r, r % 2
                        dve.wait_ge(exp_done, g + 1)
                        nc.vector.tensor_tensor(stat[:, b, 5:6], stat[:, b, 3:4], stat[:, b, 4:5], ALU.add).then_inc(p_norm, 1)
                        dve.wait_ge(p_norm, 2 * g + 1)
                        nc.vector.reciprocal(stat[:, b, 6:7], stat[:, b, 5:6]).then_inc(p_norm, 1)
                        dve.wait_ge(p_norm, 2 * g + 2)
                        nc.vector.tensor_scalar(p[:, b], p[:, b], stat[:, b, 6:7], None, ALU.mult).then_inc(p_ready, 1)
                    if i >= 3:
                        r = i - 3
                        dve.wait_ge(o_ready, ROWS * h + r + 1)
                        ps_o = score[r % 2][:, 2 * HALF:2 * HALF + P]
                        cols = slice(r * GRID_W, (r + 1) * GRID_W)
                        nc.vector.tensor_copy(o[0:HD, cols], ps_o[0:HD, 0:HD])
                        nc.vector.tensor_copy(o[HD:P, cols], ps_o[HD:P, HD:P]).then_inc(o_copied, 1)

        @block.tensor
        def _(pe):
            pe.wait_ge(consts_in, 64)
            with pe.Fori(0, PAIRS) as h:
                pe.wait_ge(o_copied, ROWS * h)
                for u, (out, n) in enumerate(((ps_a, T), (ps_b, TC))):
                    pe.wait_ge(lo_done, 2 * h + u + 1)
                    for k in range(KD):
                        for a, b in split_columns(n):
                            last = product3(nc, out[:, a:b], w_hi[:, u, k], w_lo[:, u, k], keep.h_hi.at(k, a, b), keep.h_lo.at(k, a, b),
                                            k == 0, k == KD - 1)
                    last.then_inc(proj_done, 1)
                pe.wait_ge(sq_done, 2 * h + 1)
                for a, b in split_columns(T):
                    last = nc.tensor.matmul(ps_t[:, a:b], head_ones[:], sq[:, a:b], start=True, stop=True)
                last.then_inc(sum_done, 1)
                pe.wait_ge(sq_done, 2 * h + 2)
                pe.wait_ge(q_done, 2 * h + 2)
                for a, b in split_columns(TC):
                    last = nc.tensor.matmul(ps_a[:, a:b], head_ones[:], sq[:, a:b], start=True, stop=True)
                last.then_inc(sum_done, 1)
                pe.wait_ge(k_done, h + 1)
                pe.wait_ge(v_in, 32 * (h + 1))
                for i in range(ROWS + 3):
                    if i < ROWS:
                        b = i % 2
                        if i >= 2:
                            pe.wait_ge(exp_done, ROWS * h + i - 1)
                        w0 = row0[i] * GRID_W
                        nc.tensor.matmul(score[b][:, 0:KEYS], q[:, i], k_t[:, w0:w0 + KEYS], start=True, stop=True)
                        nc.tensor.matmul(score[b][:, KEYS:ALL], q[:, i], k_t[:, T:TC], start=True, stop=True).then_inc(s_ready, 1)
                    if 2 <= i < ROWS + 2:
                        r = i - 2
                        pe.wait_ge(p_ready, ROWS * h + r + 1)
                        pe.wait_ge(t_copied, ROWS * h + r)
                        for j in range(NT):
                            last = nc.tensor.transpose(ps_t[:, j * P:(j + 1) * P], p[:, r % 2, j * P:(j + 1) * P], ident[:])
                        last.then_inc(t_ready, 1)
                    if i >= 3:
                        r = i - 3
                        pe.wait_ge(t_copied, ROWS * h + r + 1)
                        if r >= 2:
                            pe.wait_ge(o_copied, ROWS * h + r - 1)
                        tiles = v if row0[r] % 2 == 0 else v_odd
                        ps_o = score[r % 2][:, 2 * HALF:2 * HALF + P]
                        for j in range(NT):
                            v_tile = tiles[:, row0[r] // 2 + j] if j < KEYS // P else v[:, T // P + j - KEYS // P]
                            last = nc.tensor.matmul(ps_o, v_tile, p_t[:, r % 2, j], start=(j == 0), stop=(j == NT - 1))
                        last.then_inc(o_ready, 1)


CONV_W, CONV_B, BIAS, LAM = 0, 4, 5, 9
HALF_BIAS, NEG_C, HALF_C = 0, 4, 6
NVEC, NDER = 11, 8
LOG1P_TERMS = 9


def recurrence(nc, io, keep):
    GAP = CONV - 1
    U_CTX = T + GAP
    UW = U_CTX + C + 1
    ZW = UW + GAP
    with ExitStack() as ctx:
        m = Pool(nc, ctx, "r")
        raw = m.sb("raw", [P, 2, KD, P])
        w_hi = m.sb("w_hi", [P, 2, KD, P], F32R)
        w_lo = m.sb("w_lo", [P, 2, KD, P], F32R)
        gate_w = m.sb("gate_w", [P, 4, P])
        vec = m.sb("vec", [P, BLOCKS, NVEC])
        der = m.sb("der", [P, BLOCKS, NDER])
        sp_t = m.sb("sp_t", [P, 6, BLOCKS, 2])
        z = m.sb("z", [P, ZW])
        u = m.sb("u", [P, UW])
        tr = m.sb("tr", [P, 2, UW])
        ti = m.sb("ti", [P, 2, UW])
        a = m.sb("a", [P, 2, UW])
        root = m.sb("root", [P, 2, UW])
        hs = m.sb("hs", [P, 2, UW])
        gy = m.sb("gy", [P, T])
        ob = m.sb("ob", [P, T])
        ps = [m.ps("ps_a", [P, 3 * HALF]), m.ps("ps_b", [P, 3 * HALF])]
        ps_y = m.ps("ps_y", [P, T])
        vec_in, x_in, y_in, gate_in, stored = (m.sem(x) for x in ("vec_in", "x_in", "y_in", "gate_in", "stored"))
        hi_done, lo_done, x_done, y_done, g_done = (m.sem(x) for x in ("hi_done", "lo_done", "x_done", "y_done", "g_done"))
        pads, lam_abs, lam_exp, lam_step, der_done = (m.sem(x) for x in ("pads", "lam_abs", "lam_exp", "lam_step", "der_done"))
        z_done, conv_step, tanh_done, a_done, t_done, root_done, gelu_done = (m.sem(x) for x in (
            "z_done", "conv_step", "tanh_done", "a_done", "t_done", "root_done", "gelu_done"))
        iu_done, beta_done, b_done, scan_done, sum_done, ob_done = (m.sem(x) for x in (
            "iu_done", "beta_done", "b_done", "scan_done", "sum_done", "ob_done"))
        block = ctx.enter_context(nc.Block())

        def load_weights(sp, n):
            sp.dma_start(raw[:, 0], io["w_xr"][n].rearrange("p (k n) -> p k n", k=KD)).then_inc(x_in, 16)
            sp.dma_start(raw[:, 1], io["w_yr"][n].rearrange("p (k n) -> p k n", k=KD)).then_inc(y_in, 16)

        @block.sync
        def _(sp):
            sp.dma_start(vec[:], io["lru_vec"].rearrange("p (n v) -> p n v", n=BLOCKS)).then_inc(vec_in, 16)
            load_weights(sp, 0)
            with sp.Fori(0, BLOCKS) as n:
                sp.wait_ge(lo_done, 2 * n + 2)
                load_weights(sp, n + 1)
                sp.wait_ge(g_done, 4 * n)
                sp.dma_start(gate_w[:], io["w_gates"][n].rearrange("p (g n) -> p g n", g=4)).then_inc(gate_in, 16)
                sp.wait_ge(ob_done, n + 1)
                sp.dma_start(io["ob_scr"][n], ob[:]).then_inc(stored, 16)
            sp.wait_ge(stored, 16 * BLOCKS)
            sp.wait_ge(x_in, 16 * (BLOCKS + 1))
            sp.wait_ge(y_in, 16 * (BLOCKS + 1))

        @block.scalar
        def _(act):
            act.wait_ge(lam_abs, 1)
            nc.scalar.activation(sp_t[:, 1], sp_t[:, 0], ACT.Exp, scale=-1.0).then_inc(lam_exp, 1)
            act.wait_ge(x_in, 16)
            nc.scalar.activation(w_hi[:, 0], raw[:, 0], ACT.Copy).then_inc(hi_done, 1)
            act.wait_ge(y_in, 16)
            nc.scalar.activation(w_hi[:, 1], raw[:, 1], ACT.Copy).then_inc(hi_done, 1)
            act.wait_ge(der_done, 3)
            act.wait_ge(pads, 1)
            with act.Fori(0, BLOCKS) as n:
                act.wait_ge(x_done, n + 1)
                act.wait_ge(conv_step, 4 * n)
                nc.scalar.activation(z[:, CONV_LEFT:CONV_LEFT + T], ps[0][:, 0:T], ACT.Copy)
                nc.scalar.activation(z[:, U_CTX + CONV_LEFT:U_CTX + CONV_LEFT + C], ps[0][:, T:TC], ACT.Copy).then_inc(z_done, 1)
                act.wait_ge(x_in, 16 * (n + 2))
                nc.scalar.activation(w_hi[:, 0], raw[:, 0], ACT.Copy).then_inc(hi_done, 1)
                act.wait_ge(y_in, 16 * (n + 2))
                act.wait_ge(y_done, n + 1)
                nc.scalar.activation(w_hi[:, 1], raw[:, 1], ACT.Copy).then_inc(hi_done, 1)
                act.wait_ge(b_done, 2 * n)
                for j in range(4):
                    d, which = j // 2, (tr, ti)[j % 2]
                    act.wait_ge(g_done, 4 * n + j + 1)
                    nc.scalar.activation(which[:, d], ps[(j + 1) % 2][:, 0:UW], ACT.Tanh, scale=0.5,
                                         bias=der[:, bass.ds(n, 1), HALF_BIAS + j].rearrange("p a -> p a")).then_inc(tanh_done, 1)
                act.wait_ge(scan_done, 4 * n)
                for d in range(2):
                    act.wait_ge(tanh_done, 4 * n + 2 * d + 1)
                    c = der[:, bass.ds(n, 1), NEG_C + d]
                    nc.scalar.activation(a[:, d], tr[:, d], ACT.Exp, scale=c, bias=c).then_inc(a_done, 1)
                    c = der[:, bass.ds(n, 1), HALF_C + d]
                    nc.scalar.activation(root[:, d], tr[:, d], ACT.Tanh, scale=c, bias=c).then_inc(t_done, 1)
                for d in range(2):
                    act.wait_ge(t_done, 2 * n + d + 1)
                    nc.scalar.activation(root[:, d], root[:, d], ACT.Sqrt, scale=0.25).then_inc(root_done, 1)
                act.wait_ge(ob_done, n)
                nc.scalar.activation(gy[:], ps_y[:], ACT.Gelu_apprx_tanh).then_inc(gelu_done, 1)

        @block.vector
        def _(dve):
            nc.vector.memset(z[:], 0.0).then_inc(pads, 1)
            dve.wait_ge(vec_in, 16)
            nlam, e, den, q, acc, rest = (sp_t[:, i] for i in range(6))
            lam = vec[:, :, LAM:LAM + 2]
            steps = 0

            def step(instruction):
                nonlocal steps
                steps += 1
                instruction.then_inc(lam_step, 1)
                dve.wait_ge(lam_step, steps)
            step(nc.vector.tensor_scalar_mul(rest, lam, -1.0))
            nc.vector.tensor_tensor(nlam, lam, rest, ALU.max).then_inc(lam_abs, 1)
            dve.wait_ge(lam_exp, 1)
            step(nc.vector.tensor_scalar_add(den, e, 2.0))
            step(nc.vector.reciprocal(den, den))
            step(nc.vector.tensor_tensor(e, e, den, ALU.mult))
            step(nc.vector.tensor_tensor(q, e, e, ALU.mult))
            step(nc.vector.memset(acc, 1.0 / (2 * LOG1P_TERMS + 1)))
            for t in reversed(range(LOG1P_TERMS)):
                step(nc.vector.tensor_tensor(acc, acc, q, ALU.mult))
                step(nc.vector.tensor_scalar_add(acc, acc, 1.0 / (2 * t + 1)))
            step(nc.vector.tensor_tensor(acc, acc, e, ALU.mult))
            step(nc.vector.tensor_scalar_mul(acc, acc, 2.0))
            step(nc.vector.tensor_scalar_max(rest, rest, 0.0))
            step(nc.vector.tensor_tensor(acc, acc, rest, ALU.add))
            nc.vector.tensor_scalar_mul(der[:, :, NEG_C:NEG_C + 2], acc, -4.0).then_inc(der_done, 1)
            nc.vector.tensor_scalar_mul(der[:, :, HALF_C:HALF_C + 2], acc, 2.0).then_inc(der_done, 1)
            nc.vector.tensor_scalar_mul(der[:, :, HALF_BIAS:HALF_BIAS + 4], vec[:, :, BIAS:BIAS + 4], 0.5).then_inc(der_done, 1)
            for h in range(2):
                dve.wait_ge(hi_done, h + 1)
                nc.vector.tensor_tensor(w_lo[:, h], raw[:, h], w_hi[:, h].bitcast(F32), ALU.subtract).then_inc(lo_done, 1)
            with dve.Fori(0, BLOCKS) as n:
                dve.wait_ge(z_done, n + 1)
                dve.wait_ge(g_done, 4 * n)
                dve.wait_ge(iu_done, 2 * n)
                nc.vector.tensor_scalar(u[:], z[:, 0:UW], vec[:, bass.ds(n, 1), CONV_W], vec[:, bass.ds(n, 1), CONV_B], ALU.mult, ALU.add)\
                    .then_inc(conv_step, 1)
                for j in range(1, CONV):
                    dve.wait_ge(conv_step, 4 * n + j)
                    nc.vector.scalar_tensor_tensor(out=u[:], in0=z[:, j:j + UW], scalar=vec[:, bass.ds(n, 1), CONV_W + j], in1=u[:],
                                                   op0=ALU.mult, op1=ALU.add).then_inc(conv_step, 1)
                for h in range(2):
                    dve.wait_ge(hi_done, 2 * n + 3 + h)
                    nc.vector.tensor_tensor(w_lo[:, h], raw[:, h], w_hi[:, h].bitcast(F32), ALU.subtract).then_inc(lo_done, 1)
                for d in range(2):
                    dve.wait_ge(tanh_done, 4 * n + 2 * d + 2)
                    nc.vector.scalar_tensor_tensor(out=ti[:, d], in0=ti[:, d], scalar=1.0, in1=u[:], op0=ALU.add, op1=ALU.mult)\
                        .then_inc(iu_done, 1)
                for d in range(2):
                    dve.wait_ge(root_done, 2 * n + d + 1)
                    nc.vector.scalar_tensor_tensor(out=root[:, d], in0=a[:, d], scalar=1.0, in1=root[:, d], op0=ALU.add, op1=ALU.mult)\
                        .then_inc(beta_done, 1)
                for d in range(2):
                    dve.wait_ge(beta_done, 2 * n + d + 1)
                    dve.wait_ge(iu_done, 2 * n + d + 1)
                    nc.vector.tensor_tensor(ti[:, d], ti[:, d], root[:, d], ALU.mult).then_inc(b_done, 1)
                dve.wait_ge(sum_done, n)
                lat, con = slice(0, T), slice(U_CTX, U_CTX + C)
                for d, (order, end) in enumerate(((1, U_CTX + C - 1), (-1, U_CTX))):
                    dve.wait_ge(b_done, 2 * n + d + 1)
                    nc.vector.tensor_tensor_scan(hs[:, d, con][:, ::order], a[:, d, con][:, ::order], ti[:, d, con][:, ::order], 0.0,
                                                 ALU.mult, ALU.add).then_inc(scan_done, 1)
                    dve.wait_ge(scan_done, 4 * n + 2 * d + 1)
                    nc.vector.tensor_tensor_scan(hs[:, d, lat][:, ::order], a[:, d, lat][:, ::order], ti[:, d, lat][:, ::order],
                                                 hs[:, d, end:end + 1], ALU.mult, ALU.add).then_inc(scan_done, 1)
                dve.wait_ge(scan_done, 4 * n + 4)
                dve.wait_ge(stored, 16 * n)
                nc.vector.tensor_tensor(ob[:], hs[:, 0, lat], hs[:, 1, lat], ALU.add).then_inc(sum_done, 1)
                dve.wait_ge(gelu_done, n + 1)
                dve.wait_ge(sum_done, n + 1)
                nc.vector.tensor_tensor(ob[:], ob[:], gy[:], ALU.mult).then_inc(ob_done, 1)

        @block.tensor
        def _(pe):
            with pe.Fori(0, BLOCKS) as n:
                pe.wait_ge(tanh_done, 4 * n)
                for h, (out, width, done) in enumerate(((ps[0], TC, x_done), (ps_y, T, y_done))):
                    pe.wait_ge(lo_done, 2 * n + h + 1)
                    if h == 1:
                        pe.wait_ge(gelu_done, n)
                    for k in range(KD):
                        for c0, c1 in split_columns(width):
                            last = product3(nc, out[:, c0:c1], w_hi[:, h, k], w_lo[:, h, k], keep.h_hi.at(k, c0, c1), keep.h_lo.at(k, c0, c1),
                                            k == 0, k == KD - 1)
                    last.then_inc(done, 1)
                pe.wait_ge(gate_in, 16 * (n + 1))
                pe.wait_ge(conv_step, 4 * (n + 1))
                for j in range(4):
                    if j >= 2:
                        pe.wait_ge(tanh_done, 4 * n + j - 1)
                    for c0, c1 in split_columns(UW):
                        last = nc.tensor.matmul(ps[(j + 1) % 2][:, c0:c1], gate_w[:, j], u[:, c0:c1], start=True, stop=True)
                    last.then_inc(g_done, 1)


def merge(nc, io, keep):
    with ExitStack() as ctx:
        m = Pool(nc, ctx, "m")
        oa_hi, oa_lo = (m.sb(x, [P, PAIRS, T], F32R) for x in ("oa_hi", "oa_lo"))
        ob_hi, ob_lo = (m.sb(x, [P, BLOCKS, T], F32R) for x in ("ob_hi", "ob_lo"))
        raw = m.sb("raw", [P, 2, KD * P])
        w_hi = m.sb("w_hi", [P, 2, KD, P], F32R)
        w_lo = m.sb("w_lo", [P, 2, KD, P], F32R)
        part = m.sb("part", [P, 2, T])
        mg = m.sb("mg", [P, T])
        stage = m.sb("stage", [P, 2, T])
        acc = m.ps("acc", [P, 4, T])
        pieces = [("oa_scr", i, oa_hi, oa_lo) for i in range(PAIRS)] + [("ob_scr", i, ob_hi, ob_lo) for i in range(BLOCKS)]
        slots = [stage[:, 0], stage[:, 1], part[:, 0], part[:, 1], mg[:]]
        NS = len(slots)
        GROUPS = (("w_ga", KD), ("w_gb", KD), ("w_oa", PAIRS), ("w_ol", KD))
        raw_in = [m.sem(f"raw_in{b}") for b in range(2)]
        piece_in = [m.sem(f"piece_in{b}") for b in range(NS)]
        piece_hi, piece_lo, hi_done, lo_done, prod_done, sig_done, part_done, mg_done, stored = (m.sem(x) for x in (
            "piece_hi", "piece_lo", "hi_done", "lo_done", "prod_done", "sig_done", "part_done", "mg_done", "stored"))
        block = ctx.enter_context(nc.Block())

        def ahead(i, g):
            return (i, g + 2, GROUPS[g + 2]) if g < 2 else (i + 1, g - 2, GROUPS[g - 2])

        def weights(buffer, g, kd):
            return buffer[:, g % 2, 0:kd * P].rearrange("p (k n) -> p k n", n=P)

        @block.sync
        def _(sp):
            for g in range(2):
                sp.dma_start(raw[:, g], io[GROUPS[g][0]][0]).then_inc(raw_in[g], 16)
            for n, (name, i, _, _) in enumerate(pieces):
                if n >= NS:
                    sp.wait_ge(piece_lo, n - NS + 1)
                sp.dma_start(slots[n % NS], io[name][i]).then_inc(piece_in[n % NS], 16)
            with sp.Fori(0, KD) as i:
                for g in range(4):
                    step, g2, (name, kd) = ahead(i, g)
                    sp.wait_ge(lo_done, 4 * i + g + 1)
                    sp.dma_start(raw[:, g2 % 2, 0:kd * P], io[name][step]).then_inc(raw_in[g2 % 2], 16)
                sp.wait_ge(mg_done, i + 1)
                sp.dma_start(io["mg_scr"][i], mg[:]).then_inc(stored, 16)
            sp.wait_ge(stored, 16 * KD)
            for b in range(2):
                sp.wait_ge(raw_in[b], 16 * (2 * KD + 1))

        @block.scalar
        def _(act):
            def high(g, kd, count):
                act.wait_ge(raw_in[g % 2], count)
                nc.scalar.activation(w_hi[:, g % 2, 0:kd], weights(raw, g, kd), ACT.Copy).then_inc(hi_done, 1)

            for g in range(2):
                high(g, KD, 16)
            for n, (_, i, hi, _) in enumerate(pieces):
                act.wait_ge(piece_in[n % NS], 16 * (n // NS + 1))
                nc.scalar.activation(hi[:, i], slots[n % NS], ACT.Copy).then_inc(piece_hi, 1)
            with act.Fori(0, KD) as i:
                for g in range(4):
                    _, g2, (_, kd) = ahead(i, g)
                    act.wait_ge(prod_done, 4 * i + g + 1)
                    if g < 2:
                        act.wait_ge(mg_done, i)
                        if g == 0:
                            act.wait_ge(piece_lo, len(pieces))
                        nc.scalar.activation(part[:, g], acc[:, g], ACT.Sigmoid).then_inc(sig_done, 1)
                    high(g2, kd, 32 * i + 16 * (g // 2 + 2))

        @block.vector
        def _(dve):
            def low(g, kd, count):
                dve.wait_ge(hi_done, count)
                nc.vector.tensor_tensor(w_lo[:, g % 2, 0:kd], weights(raw, g, kd), w_hi[:, g % 2, 0:kd].bitcast(F32), ALU.subtract)\
                    .then_inc(lo_done, 1)

            for g in range(2):
                low(g, KD, g + 1)
            for n, (_, i, hi, lo) in enumerate(pieces):
                dve.wait_ge(piece_hi, n + 1)
                nc.vector.tensor_tensor(lo[:, i], slots[n % NS], hi[:, i].bitcast(F32), ALU.subtract).then_inc(piece_lo, 1)
            with dve.Fori(0, KD) as i:
                for g in range(4):
                    _, g2, (_, kd) = ahead(i, g)
                    low(g2, kd, 4 * i + g + 3)
                    if g >= 2:
                        dve.wait_ge(prod_done, 4 * i + g + 1)
                        dve.wait_ge(sig_done, 2 * i + g - 1)
                        nc.vector.tensor_tensor(part[:, g - 2], part[:, g - 2], acc[:, g], ALU.mult).then_inc(part_done, 1)
                dve.wait_ge(part_done, 2 * i + 2)
                dve.wait_ge(stored, 16 * i)
                nc.vector.tensor_tensor(mg[:], part[:, 0], part[:, 1], ALU.add).then_inc(mg_done, 1)

        @block.tensor
        def _(pe):
            with pe.Fori(0, KD) as i:
                for g, (_, kd) in enumerate(GROUPS):
                    pe.wait_ge(lo_done, 4 * i + g + 1)
                    if g < 2:
                        pe.wait_ge(sig_done, 2 * i)
                    else:
                        pe.wait_ge(part_done, 2 * i)
                        pe.wait_ge(piece_lo, len(pieces))
                    for k in range(kd):
                        for a, b in split_columns(T):
                            if g < 2:
                                hi, lo = keep.h_hi.at(k, a, b), keep.h_lo.at(k, a, b)
                            elif g == 2:
                                hi, lo = oa_hi[:, k, a:b], oa_lo[:, k, a:b]
                            else:
                                hi, lo = ob_hi[:, k, a:b], ob_lo[:, k, a:b]
                            last = product3(nc, acc[:, g, a:b], w_hi[:, g % 2, k], w_lo[:, g % 2, k], hi, lo, k == 0, k == kd - 1)
                    last.then_inc(prod_done, 1)


def project(nc, io, keep):
    with ExitStack() as ctx:
        m = Pool(nc, ctx, "p")
        mg_hi, mg_lo = (m.sb(x, [P, KD, T], F32R) for x in ("mg_hi", "mg_lo"))
        raw = m.sb("raw", [P, 2, KD * P])
        w_hi = m.sb("w_hi", [P, 2, KD, P], F32R)
        w_lo = m.sb("w_lo", [P, 2, KD, P], F32R)
        x = m.sb("x", [P, 2, T])
        x1 = m.sb("x1", [P, KD, T])
        sq = m.sb("sq", [P, T])
        total = m.sb("total", [P, T])
        ones = m.sb("ones", [P, P])
        eps = m.sb("eps", [P, 1])
        acc = m.ps("acc", [P, 2, T])
        ps_sum = m.ps("ps_sum", [P, T])
        raw_in = [m.sem(f"raw_in{b}") for b in range(2)]
        x_in = [m.sem(f"x_in{b}") for b in range(2)]
        mg_in = [m.sem(f"mg_in{b}") for b in range(KD)]
        mg_hi_done, mg_lo_done, hi_done, lo_done, prod_done, x1_done, stored = (m.sem(s) for s in (
            "mg_hi_done", "mg_lo_done", "hi_done", "lo_done", "prod_done", "x1_done", "stored"))
        consts, sq_done, sq_added, sq_summed, root_done, rstd_done, normed, modulated, h2_hi_done, h2_lo_done = (m.sem(s) for s in (
            "consts", "sq_done", "sq_added", "sq_summed", "root_done", "rstd_done", "normed", "modulated", "h2_hi_done", "h2_lo_done"))
        block = ctx.enter_context(nc.Block())

        def weights(buffer, b):
            return buffer[:, b].rearrange("p (k n) -> p k n", n=P)

        @block.sync
        def _(sp):
            for b in range(2):
                sp.dma_start(raw[:, b], io["w_out"][b]).then_inc(raw_in[b], 16)
            for n in range(KD):
                sp.dma_start(x1[:, n], io["mg_scr"][n]).then_inc(mg_in[n], 16)
            with sp.Fori(0, KD // 2) as i:
                for b in range(2):
                    x_col = sp.snap((2 * i + b) * T)
                    sp.wait_ge(x1_done, 2 * i + b + 1)
                    sp.dma_start(x[:, b], io["xt"][:, bass.ds(x_col, T)]).then_inc(x_in[b], 16)
                    sp.wait_ge(lo_done, 2 * i + b + 1)
                    sp.dma_start(raw[:, b], io["w_out"][2 * i + (2 + b)]).then_inc(raw_in[b], 16)
            for n in range(KD):
                sp.wait_ge(x1_done, 2 + n + 1)
                sp.dma_start(io["x1_scr"][n], x1[:, n]).then_inc(stored, 16)
            sp.wait_ge(stored, 16 * KD)

        @block.scalar
        def _(act):
            for b in range(2):
                act.wait_ge(raw_in[b], 16)
                nc.scalar.activation(w_hi[:, b], weights(raw, b), ACT.Copy).then_inc(hi_done, 1)
            for n in range(KD):
                act.wait_ge(mg_in[n], 16)
                nc.scalar.activation(mg_hi[:, n], x1[:, n], ACT.Copy).then_inc(mg_hi_done, 1)
            with act.Fori(0, KD // 2) as i:
                for b in range(2):
                    act.wait_ge(raw_in[b], 16 * i + 32)
                    act.wait_ge(prod_done, 2 * i + b + 1)
                    nc.scalar.activation(w_hi[:, b], weights(raw, b), ACT.Copy).then_inc(hi_done, 1)
                    act.wait_ge(x1_done, 2 * i + b + 3)
                    act.wait_ge(sq_added, 2 * i + b + 1)
                    nc.scalar.activation(sq[:].rearrange("p (a t) -> p a t", a=1), x1[:, bass.ds(2 * i + b, 1)], ACT.Square).then_inc(sq_done, 1)
            act.wait_ge(sq_summed, 1)
            nc.scalar.activation(x[:, 0], ps_sum[:], ACT.Sqrt, bias=eps[:], scale=1.0 / D).then_inc(root_done, 1)
            for k in range(KD):
                act.wait_ge(modulated, k + 1)
                nc.scalar.activation(keep.h2_hi[:, k], x1[:, k], ACT.Copy).then_inc(h2_hi_done, 1)

        @block.vector
        def _(dve):
            def low(b, count):
                dve.wait_ge(hi_done, count)
                nc.vector.tensor_tensor(w_lo[:, b], weights(raw, b), w_hi[:, b].bitcast(F32), ALU.subtract).then_inc(lo_done, 1)

            nc.vector.memset(ones[:], 1.0).then_inc(consts, 1)
            nc.vector.memset(eps[:], EPS).then_inc(consts, 1)
            nc.vector.memset(total[:], 0.0).then_inc(sq_added, 1)
            dve.sem_inc(x1_done, 2)
            for b in range(2):
                low(b, b + 1)
            for n in range(KD):
                dve.wait_ge(mg_hi_done, n + 1)
                nc.vector.tensor_tensor(mg_lo[:, n], x1[:, n], mg_hi[:, n].bitcast(F32), ALU.subtract).then_inc(mg_lo_done, 1)
            dve.wait_ge(mg_lo_done, KD)
            with dve.Fori(0, KD // 2) as i:
                for b in range(2):
                    low(b, 2 * i + b + 3)
                    dve.wait_ge(prod_done, 2 * i + b + 1)
                    dve.wait_ge(x_in[b], 16 * (i + 1))
                    nc.vector.scalar_tensor_tensor(out=x1[:, bass.ds(2 * i + b, 1)], in0=acc[:, b:b + 1], scalar=keep.mod[:, bass.ds(2 * i + (2 * KD + b), 1)],
                                                   in1=x[:, b:b + 1], op0=ALU.mult, op1=ALU.add).then_inc(x1_done, 1)
                    dve.wait_ge(sq_done, 2 * i + b + 1)
                    dve.wait_ge(sq_added, 2 * i + b + 1)
                    nc.vector.tensor_tensor(total[:], total[:], sq[:], ALU.add).then_inc(sq_added, 1)
            dve.wait_ge(root_done, 1)
            nc.vector.reciprocal(x[:, 1], x[:, 0]).then_inc(rstd_done, 1)
            dve.wait_ge(rstd_done, 1)
            for k in range(KD):
                dve.wait_ge(stored, 16 * KD)
                nc.vector.tensor_tensor(x1[:, k], x1[:, k], x[:, 1], ALU.mult).then_inc(normed, 1)
                if k >= 1:
                    dve.wait_ge(normed, k)
                    nc.vector.tensor_scalar(x1[:, k - 1], x1[:, k - 1], keep.gain[:, 2, k - 1:k], keep.mod[:, 3 * KD + k - 1:3 * KD + k],
                                            ALU.mult, ALU.add).then_inc(modulated, 1)
            dve.wait_ge(normed, KD)
            nc.vector.tensor_scalar(x1[:, KD - 1], x1[:, KD - 1], keep.gain[:, 2, KD - 1:KD], keep.mod[:, 4 * KD - 1:4 * KD], ALU.mult, ALU.add)\
                .then_inc(modulated, 1)
            for k in range(KD):
                dve.wait_ge(h2_hi_done, k + 1)
                nc.vector.tensor_tensor(keep.h2_lo[:, k], x1[:, k], keep.h2_hi[:, k].bitcast(F32), ALU.subtract).then_inc(h2_lo_done, 1)

        @block.tensor
        def _(pe):
            pe.wait_ge(mg_lo_done, KD)
            with pe.Fori(0, KD // 2) as i:
                for b in range(2):
                    pe.wait_ge(lo_done, 2 * i + b + 1)
                    pe.wait_ge(x1_done, 2 * i + b + 1)
                    for k in range(KD):
                        for c0, c1 in split_columns(T):
                            last = product3(nc, acc[:, b, c0:c1], w_hi[:, b, k], w_lo[:, b, k], mg_hi[:, k, c0:c1], mg_lo[:, k, c0:c1],
                                            k == 0, k == KD - 1)
                    last.then_inc(prod_done, 1)
            pe.wait_ge(consts, 2)
            pe.wait_ge(sq_added, KD + 1)
            for c0, c1 in split_columns(T):
                last = nc.tensor.matmul(ps_sum[:, c0:c1], ones[:], total[:, c0:c1], start=True, stop=True)
            last.then_inc(sq_summed, 1)


def hold(eng, semaphore, value, passed):
    eng.wait_ge(semaphore, value)
    eng.sem_inc(passed, 1)


USED = -3e38


def top16(nc, dve, n, values, scratch, best, place, done, base, passed):
    for i in range(n):
        nc.vector.max(best(i, 0), values(i)).then_inc(done, 1)
    hold(dve, done, base + n, passed)
    for i in range(n):
        nc.vector.match_replace(scratch(i), best(i, 0), values(i), USED).then_inc(done, 1)
    for i in range(n):
        nc.vector.max_index(place(i, 0), best(i, 0), values(i)).then_inc(done, 1)
    hold(dve, done, base + 2 * n, passed)
    for i in range(n):
        nc.vector.max(best(i, 1), scratch(i)).then_inc(done, 1)
    hold(dve, done, base + 4 * n, passed)
    for i in range(n):
        nc.vector.max_index(place(i, 1), best(i, 1), scratch(i)).then_inc(done, 1)


def route(nc, io, keep):
    UNITS = 2 * PH
    with ExitStack() as ctx:
        m = Pool(nc, ctx, "q")
        raw = m.sb("raw", [P, 2, KD, P])
        w_hi = m.sb("w_hi", [P, 2, KD, P], F32R)
        w_lo = m.sb("w_lo", [P, 2, KD, P], F32R)
        keys = m.sb("keys", [P, UNITS, NK])
        q = m.sb("q", [P, 2, T])
        struck = m.sb("struck", [P, TT, NK])
        best = m.sb("best", [P, TT, TOPK])
        place = m.sb("place", [P, TT, TOPK], U32)
        acc = m.ps("acc", [P, 2, T])
        score = m.ps("score", [P, 2, T])
        raw_in = [m.sem(f"raw_in{b}") for b in range(2)]
        keys_in, hi_done, lo_done, half_done, q_done, s_ready, top_done, kept, passed = (m.sem(x) for x in (
            "keys_in", "hi_done", "lo_done", "half_done", "q_done", "s_ready", "top_done", "kept", "passed"))
        block = ctx.enter_context(nc.Block())

        @block.sync
        def _(sp):
            sp.dma_start(keys[:], io["keys"].rearrange("p (u n) -> p u n", u=UNITS)).then_inc(keys_in, 16)
            with sp.Fori(0, UNITS // 2) as i:
                for b in range(2):
                    sp.wait_ge(lo_done, 2 * i + b + 1)
                    sp.dma_start(raw[:, b], io["w_pq"][2 * i + b].rearrange("p (k n) -> p k n", k=KD)).then_inc(raw_in[b], 16)
            sp.wait_ge(lo_done, UNITS + 1)
            sp.dma_start(raw[:, 0], io["w_pq"][UNITS].rearrange("p (k n) -> p k n", k=KD)).then_inc(raw_in[0], 16)

        @block.scalar
        def _(act):
            act.wait_ge(raw_in[0], 16)
            nc.scalar.activation(w_hi[:, 0], raw[:, 0], ACT.Copy).then_inc(hi_done, 1)
            with act.Fori(0, UNITS // 2) as i:
                for b in range(2):
                    nb = 1 - b
                    act.wait_ge(raw_in[nb], 16 * (i + 1 + b))
                    act.wait_ge(half_done, 4 * i + 2 * b)
                    nc.scalar.activation(w_hi[:, nb], raw[:, nb], ACT.Copy).then_inc(hi_done, 1)
                    act.wait_ge(s_ready, 2 * i + b)
                    for c, (c0, c1) in enumerate(split_columns(T)):
                        act.wait_ge(half_done, 4 * i + 2 * b + c + 1)
                        nc.scalar.activation(q[:, b, c0:c1], acc[:, b, c0:c1], ACT.Copy).then_inc(q_done, 1)

        @block.vector
        def _(dve):
            dve.sem_inc(lo_done, 2)
            dve.wait_ge(hi_done, 1)
            nc.vector.tensor_tensor(w_lo[:, 0], raw[:, 0], w_hi[:, 0].bitcast(F32), ALU.subtract).then_inc(lo_done, 1)
            with dve.Fori(0, UNITS // 2) as i:
                for b in range(2):
                    nb = 1 - b
                    dve.wait_ge(hi_done, 2 * i + b + 2)
                    nc.vector.tensor_tensor(w_lo[:, nb], raw[:, nb], w_hi[:, nb].bitcast(F32), ALU.subtract).then_inc(lo_done, 1)
                    hold(dve, kept, 4 * i + 2 * b, passed)
                    hold(dve, s_ready, 2 * i + b + 1, passed)
                    s = score[:, b].rearrange("p (t n) -> p t n", t=TT)
                    top16(nc, dve, TT, lambda t: s[:, t], lambda t: struck[:, t], lambda t, g: best[:, t, 8 * g:8 * g + 8],
                          lambda t, g: place[:, t, 8 * g:8 * g + 8], top_done, (2 * i + b) * (5 * TT), passed)
                    dve.wait_ge(top_done, (2 * i + b + 1) * (5 * TT))
                    unit = bass.ds(2 * i + b, 1)
                    nc.vector.tensor_copy(keep.best[:, :, unit], best[:].rearrange("p t (u n) -> p t u n", u=1)).then_inc(kept, 1)
                    nc.vector.tensor_copy(keep.place[:, :, unit], place[:].rearrange("p t (u n) -> p t u n", u=1)).then_inc(kept, 1)

        @block.tensor
        def _(pe):
            pe.wait_ge(keys_in, 16)
            with pe.Fori(0, UNITS // 2) as i:
                for b in range(2):
                    pe.wait_ge(lo_done, 2 * i + b + 3)
                    pe.wait_ge(q_done, 4 * i + 2 * b)
                    for c0, c1 in split_columns(T):
                        for k in range(KD):
                            last = product3(nc, acc[:, b, c0:c1], w_hi[:, b, k], w_lo[:, b, k], keep.h2_hi[:, k, c0:c1], keep.h2_lo[:, k, c0:c1],
                                            k == 0, k == KD - 1)
                        last.then_inc(half_done, 1)
                    pe.wait_ge(top_done, (2 * i + b) * (5 * TT))
                    for t in range(TT):
                        pe.wait_ge(q_done, 4 * i + 2 * b + t // (TT // 2) + 1)
                        last = nc.tensor.matmul(score[:, b, t * NK:(t + 1) * NK], q[:, b, t * P:(t + 1) * P],
                                                keys[:, bass.ds(2 * i + b, 1)].rearrange("p u n -> p (u n)"), start=True, stop=True)
                    last.then_inc(s_ready, 1)


def gates(nc, io, keep):
    SEL = PH * TOPK
    WHOLE = 4
    CUT = TOPK // WHOLE
    CAND = WHOLE * TOPK + (TOPK - WHOLE) * CUT
    GT = 8
    GROUPS = P // GT
    with ExitStack() as ctx:
        m = Pool(nc, ctx, "g")
        iota = m.sb("iota", [P, NK])
        ident = m.sb("ident", [P, P])
        va = m.sb("va", [P, 2 * PH, TOPK])
        xa = m.sb("xa", [P, 2 * PH, TOPK])
        cand = m.sb("cand", [P, PH, CAND])
        struck = m.sb("struck", [P, PH, CAND])
        best = m.sb("best", [P, PH, TOPK])
        pos = m.sb("pos", [P, SEL], U32)
        shifted = m.sb("shifted", [P, 2, SEL], U32)
        digit = m.sb("digit", [P, 2, SEL])
        start = m.sb("start", [P, 2, SEL])
        hit = m.sb("hit", [P, 2, SEL, TOPK])
        total = m.sb("total", [P, PH])
        sel = m.sb("sel", [P, 3, SEL])
        sel_t = m.sb("sel_t", [P, 3, P])
        one2 = m.sb("one2", [P, 2, GT, NK])
        one1 = m.sb("one1", [P, 2, GT, NK])
        gm = m.sb("gm", [P, NK, P])
        ps_t = m.ps("ps_t", [P, HALF])
        ps_g = m.ps("ps_g", [P, 2, GT * NK])
        consts_in, top_done, passed, step, second_hit, exp_done, t_ready, oh_done, g_ready, g_copied, stored, hot_done, pool_passed = (m.sem(x) for x in (
            "consts_in", "top_done", "passed", "step", "second_hit", "exp_done", "t_ready", "oh_done", "g_ready", "g_copied", "stored", "hot_done", "pool_passed"))
        STEPS = 20
        block = ctx.enter_context(nc.Block())

        SECOND = 12
        places = iota[:, 0:TOPK].rearrange("p (o a) -> p o a", o=1).broadcast_to([P, SEL, TOPK])

        def choice(s):
            return digit[:, s].rearrange("p (n o) -> p n o", o=1).broadcast_to([P, SEL, TOPK])

        @block.sync
        def _(sp):
            sp.dma_start(iota[:], io["iota"]).then_inc(consts_in, 16)
            sp.dma_start(ident[:], io["ident"]).then_inc(consts_in, 16)
            with sp.Fori(0, TT) as tt:
                col = sp.snap(tt * P)
                sp.wait_ge(g_copied, GROUPS * (tt + 1) + 2)
                sp.dma_start(io["gm_scr"][:, :, bass.ds(col, P)].rearrange("i p t -> p i t"), gm[:]).then_inc(stored, 16)
            sp.wait_ge(stored, 16 * TT)

        @block.scalar
        def _(act):
            act.sem_inc(g_copied, 2)
            with act.Fori(0, TT) as tt:
                act.wait_ge(step, STEPS * tt + 5)
                nc.scalar.activation(best[:], best[:], ACT.Exp).then_inc(exp_done, 1)
                act.wait_ge(stored, 16 * tt)
                with act.Fori(0, GROUPS // 2) as i:
                    for b in range(2):
                        act.wait_ge(g_ready, GROUPS * tt + 2 * i + b + 2)
                        nc.scalar.activation(gm[:, :, bass.ds(2 * GT * i + GT * b, GT)].rearrange("p i t -> p t i"),
                                             ps_g[:, b].rearrange("p (t i) -> p t i", t=GT), ACT.Copy).then_inc(g_copied, 1)

        @block.vector
        def _(dve):
            dve.wait_ge(consts_in, 32)
            with dve.Fori(0, TT) as tt:
                done = 0

                def then(instruction):
                    nonlocal done
                    done += 1
                    instruction.then_inc(step, 1)

                def ready(n=None):
                    dve.wait_ge(step, STEPS * tt + (done if n is None else n))

                then(nc.vector.tensor_copy(va[:], keep.best[:, bass.ds(tt, 1)].rearrange("p a u n -> p (a u) n")))
                then(nc.vector.tensor_copy(xa[:], keep.place[:, bass.ds(tt, 1)].rearrange("p a u n -> p (a u) n")))
                ready()
                v4 = va[:].rearrange("p (h s) k -> p h s k", s=2)
                x4 = xa[:].rearrange("p (h s) k -> p h s k", s=2)
                grid = [P, PH, TOPK, TOPK]
                for a0, a1, cols, c0 in ((0, WHOLE, TOPK, 0), (WHOLE, TOPK, CUT, WHOLE * TOPK)):
                    part = [P, PH, a1 - a0, cols]
                    then(nc.vector.tensor_tensor(
                        cand[:, :, c0:c0 + (a1 - a0) * cols].rearrange("p h (a b) -> p h a b", b=cols),
                        v4[:, :, 0, a0:a1].rearrange("p h (a o) -> p h a o", o=1).broadcast_to(part),
                        v4[:, :, 1, 0:cols].rearrange("p h (o b) -> p h o b", o=1).broadcast_to(part), ALU.add))
                hold(dve, step, STEPS * tt + done, passed)
                top16(nc, dve, PH, lambda h: cand[:, h], lambda h: struck[:, h], lambda h, g: best[:, h, 8 * g:8 * g + 8],
                      lambda h, g: pos[:, h * TOPK + 8 * g:h * TOPK + 8 * g + 8], top_done, tt * (5 * PH), passed)
                dve.wait_ge(top_done, (tt + 1) * (5 * PH))
                then(nc.vector.tensor_tensor(best[:], best[:], cand[:, :, 0:1].broadcast_to([P, PH, TOPK]), ALU.subtract))
                then(nc.vector.tensor_scalar(shifted[:, 0], pos[:], 4, None, ALU.logical_shift_right))
                then(nc.vector.tensor_scalar(shifted[:, 1], pos[:], 2, None, ALU.logical_shift_right))
                ready()
                then(nc.vector.scalar_tensor_tensor(out=digit[:, 0], in0=shifted[:, 1], scalar=float(WHOLE - WHOLE * TOPK // CUT), in1=shifted[:, 0],
                                                    op0=ALU.add, op1=ALU.max))
                ready()
                then(nc.vector.tensor_scalar(start[:, 0], digit[:, 0], float(CUT), float(WHOLE * (TOPK - CUT)), ALU.mult, ALU.add))
                ready()
                then(nc.vector.scalar_tensor_tensor(out=start[:, 1], in0=digit[:, 0], scalar=float(TOPK), in1=start[:, 0],
                                                    op0=ALU.mult, op1=ALU.min))
                ready()
                then(nc.vector.tensor_tensor(digit[:, 1], pos[:], start[:, 1], ALU.subtract))
                ready()
                then(nc.vector.tensor_tensor(hit[:, 1], choice(1), places, ALU.is_equal))
                assert done == SECOND, done
                then(nc.vector.tensor_tensor(hit[:, 0], choice(0), places, ALU.is_equal))
                ready()
                h4 = hit[:, 0].rearrange("p (h k) a -> p h k a", h=PH)
                then(nc.vector.tensor_tensor(h4, h4, x4[:, :, 0].rearrange("p h (o a) -> p h o a", o=1).broadcast_to(grid), ALU.mult))
                ready()
                then(nc.vector.reduce_sum(sel[:, 0], hit[:, 0], AX_X))
                dve.wait_ge(exp_done, tt + 1)
                then(nc.vector.reduce_sum(total[:], best[:], AX_X))
                ready()
                then(nc.vector.reciprocal(total[:], total[:]))
                ready()
                then(nc.vector.tensor_tensor(sel[:, 2].rearrange("p (h k) -> p h k", h=PH), best[:],
                                             total[:].rearrange("p (h o) -> p h o", o=1).broadcast_to([P, PH, TOPK]), ALU.mult))
                dve.wait_ge(second_hit, tt + 1)
                then(nc.vector.reduce_sum(sel[:, 1], hit[:, 1], AX_X))
                dve.wait_ge(t_ready, tt + 1)
                dve.wait_ge(oh_done, GROUPS * tt)
                then(nc.vector.tensor_copy(sel_t[:], ps_t[:, 0:3 * P].rearrange("p (a t) -> p a t", a=3)))
                hold(dve, step, STEPS * tt + done, passed)
                assert done == STEPS, done
                block8 = [P, GT, NK]
                columns = iota[:].rearrange("p (o n) -> p o n", o=1).broadcast_to(block8)
                with dve.Fori(0, GROUPS // 2) as i:
                    for b in range(2):
                        dve.wait_ge(g_ready, GROUPS * tt + 2 * i + b)
                        for a, one in ((1, one2), (0, one1)):
                            key = sel_t[:, a, bass.ds(2 * GT * i + GT * b, GT)].rearrange("p (t o) -> p t o", o=1).broadcast_to(block8)
                            last = nc.vector.tensor_tensor(one[:, b], columns, key, ALU.is_equal)
                        last.then_inc(hot_done, 1)

        @block.gpsimd
        def _(pool):
            with pool.Fori(0, TT) as tt:
                hold(pool, step, STEPS * tt + SECOND, pool_passed)
                h4 = hit[:, 1].rearrange("p (h k) a -> p h k a", h=PH)
                x = xa[:].rearrange("p (h s) k -> p h s k", s=2)[:, :, 1].rearrange("p h (o a) -> p h o a", o=1).broadcast_to([P, PH, TOPK, TOPK])
                nc.gpsimd.tensor_tensor(h4, h4, x, ALU.mult).then_inc(second_hit, 1)
                with pool.Fori(0, GROUPS // 2) as i:
                    for b in range(2):
                        gate = sel_t[:, 2, bass.ds(2 * GT * i + GT * b, GT)].rearrange("p (t o) -> p t o", o=1).broadcast_to([P, GT, NK])
                        hold(pool, hot_done, GROUPS * tt + 2 * i + b + 1, pool_passed)
                        nc.gpsimd.tensor_tensor(one1[:, b], one1[:, b], gate, ALU.mult).then_inc(oh_done, 1)

        @block.tensor
        def _(pe):
            pe.wait_ge(consts_in, 32)
            pe.sem_inc(g_ready, 1)
            with pe.Fori(0, TT) as tt:
                pe.wait_ge(step, STEPS * tt + STEPS - 1)
                for a in range(3):
                    last = nc.tensor.transpose(ps_t[:, a * P:(a + 1) * P], sel[:, a], ident[:])
                last.then_inc(t_ready, 1)
                with pe.Fori(0, GROUPS // 2) as i:
                    for b in range(2):
                        pe.wait_ge(oh_done, GROUPS * tt + 2 * i + b + 1)
                        pe.wait_ge(g_copied, GROUPS * tt + 2 * i + b + 1)
                        for j in range(GT):
                            out = ps_g[:, b, j * NK:(j + 1) * NK]
                            last = nc.tensor.matmul(out, one2[:, b, j], one1[:, b, j], start=True, stop=True)
                        last.then_inc(g_ready, 1)


def experts(nc, io, keep):
    CHUNKS = NK
    PIECES = 2 * KD
    with ExitStack() as ctx:
        m = Pool(nc, ctx, "e")
        y = m.sb("y", [P, KD, T])
        u_raw = m.sb("u_raw", [P, 2, KD, P])
        u_hi = m.sb("u_hi", [P, 2, KD, P], F32R)
        u_lo = m.sb("u_lo", [P, 2, KD, P], F32R)
        v_raw = m.sb("v_raw", [P, 2, D])
        v_hi = m.sb("v_hi", [P, 4, D], F32R)
        v_lo = m.sb("v_lo", [P, 4, D], F32R)
        g = m.sb("g", [P, 2, T])
        a = m.sb("a", [P, T])
        wa_hi = m.sb("wa_hi", [P, 4, T], F32R)
        wa_lo = m.sb("wa_lo", [P, 4, T], F32R)
        ps_a = m.ps("ps_a", [P, 2, T])
        ps_y = m.ps("ps_y", [P, 4, HALF])
        u_in, v_in, g_in = ([m.sem(f"{x}{b}") for b in range(2)] for x in ("u_in", "v_in", "g_in"))
        u_hi_done, u_lo_done, v_hi_done, v_lo_done, wa_hi_done, wa_lo_done = (m.sem(x) for x in (
            "u_hi_done", "u_lo_done", "v_hi_done", "v_lo_done", "wa_hi_done", "wa_lo_done"))
        a_ready, act_done, gated, y_ready, y_added, x1_in, out_done, stored = (m.sem(x) for x in (
            "a_ready", "act_done", "gated", "y_ready", "y_added", "x1_in", "out_done", "stored"))
        PAIR = PIECES
        block = ctx.enter_context(nc.Block())

        @block.sync
        def _(sp):
            def load(name, c, ring, slot, sems, free):
                sp.wait_ge(free, c + 1)
                dst = ring[:, slot]
                src = io[name][c]
                if name == "u":
                    src = src.rearrange("p (k n) -> p k n", k=KD)
                sp.dma_start(dst, src).then_inc(sems[slot], 16)

            load("u", 0, u_raw, 0, u_in, u_lo_done)
            load("u", 1, u_raw, 1, u_in, u_lo_done)
            with sp.Fori(0, CHUNKS // 2) as p:
                for s in range(2):
                    load("v", 2 * p + s, v_raw, s, v_in, v_lo_done)
                    load("gm_scr", 2 * p + s, g, s, g_in, wa_lo_done)
                    load("u", 2 * p + 2 + s, u_raw, s, u_in, u_lo_done)
            sp.wait_ge(u_in[0], 16 * (CHUNKS // 2 + 1))
            sp.wait_ge(u_in[1], 16 * (CHUNKS // 2 + 1))
            for k in range(KD):
                if k < 2:
                    sp.wait_ge(v_lo_done, CHUNKS + 2)
                else:
                    sp.wait_ge(out_done, k - 1)
                sp.dma_start(v_raw[:, k % 2], io["x1_scr"][k]).then_inc(x1_in, 16)
                if k >= 1:
                    sp.wait_ge(out_done, k)
                    sp.dma_start(io["out"][:, (k - 1) * T:k * T], y[:, k - 1]).then_inc(stored, 16)
                sp.wait_ge(x1_in, 16 * (k + 1))
            sp.wait_ge(out_done, KD)
            sp.dma_start(io["out"][:, (KD - 1) * T:KD * T], y[:, KD - 1]).then_inc(stored, 16)
            sp.wait_ge(stored, 16 * KD)

        @block.scalar
        def _(act):
            def split_u(c, s):
                act.wait_ge(u_in[s], 16 * (c // 2 + 1) if isinstance(c, int) else 16 * c[0] + 16)
                c = c if isinstance(c, int) else 2 * c[0] + c[1]
                act.wait_ge(a_ready, c + 1)
                nc.scalar.activation(u_hi[:, s], u_raw[:, s], ACT.Copy).then_inc(u_hi_done, 1)

            def activate(p, s, r):
                c = 2 * p + s
                act.wait_ge(a_ready, c + 3)
                act.wait_ge(gated, c)
                nc.scalar.activation(a[:], ps_a[:, s], ACT.Gelu_apprx_tanh).then_inc(act_done, 1)
                act.wait_ge(gated, c + 1)
                nc.scalar.activation(wa_hi[:, r], g[:, s], ACT.Copy).then_inc(wa_hi_done, 1)

            act.sem_inc(act_done, 2)
            split_u(0, 0)
            split_u(1, 1)
            with act.Fori(0, CHUNKS // 4) as i:
                for h in range(2):
                    p = 2 * i + h
                    act.wait_ge(y_ready, PAIR * p + PAIR)
                    for s in range(2):
                        act.wait_ge(v_in[s], 16 * p + 16)
                        nc.scalar.activation(v_hi[:, 2 * h + s], v_raw[:, s], ACT.Copy).then_inc(v_hi_done, 1)
                    split_u((p + 1, 0), 0)
                    activate(p, 0, 2 * h)
                    activate(p, 1, 2 * h + 1)
                    split_u((p + 1, 1), 1)

        @block.vector
        def _(dve):
            def lo(dst, raw, hi, hi_done, count, done):
                dve.wait_ge(hi_done, count)
                nc.vector.tensor_tensor(dst, raw, hi.bitcast(F32), ALU.subtract).then_inc(done, 1)

            def step(p, h, add):
                for s in range(2):
                    lo(v_lo[:, 2 * h + s], v_raw[:, s], v_hi[:, 2 * h + s], v_hi_done, 2 * p + s + 1, v_lo_done)
                lo(u_lo[:, 0], u_raw[:, 0], u_hi[:, 0], u_hi_done, 2 * p + 3, u_lo_done)
                for s in range(2):
                    c = 2 * p + s
                    dve.wait_ge(g_in[s], 16 * p + 16)
                    dve.wait_ge(act_done, c + 3)
                    nc.vector.tensor_tensor(g[:, s], g[:, s], a[:], ALU.mult).then_inc(gated, 1)
                    lo(wa_lo[:, 2 * h + s], g[:, s], wa_hi[:, 2 * h + s], wa_hi_done, c + 1, wa_lo_done)
                lo(u_lo[:, 1], u_raw[:, 1], u_hi[:, 1], u_hi_done, 2 * p + 4, u_lo_done)
                if add:
                    add_pair(p - 1)

            def add_pair(p):
                dve.wait_ge(y_added, PAIR * p + 4)
                for j in range(PIECES):
                    out = y[:, j // 2, (j % 2) * HALF:(j % 2 + 1) * HALF]
                    dve.wait_ge(y_ready, PAIR * p + (2 * PAIR + j + 1))
                    nc.vector.tensor_tensor(out, out, ps_y[:, j % 4], ALU.add).then_inc(y_added, 1)

            for sem in (u_lo_done, v_lo_done, wa_lo_done):
                dve.sem_inc(sem, 2)
            nc.vector.memset(y[:], 0.0).then_inc(y_added, 4)
            for s in range(2):
                lo(u_lo[:, s], u_raw[:, s], u_hi[:, s], u_hi_done, s + 1, u_lo_done)
            step(0, 0, False)
            step(1, 1, True)
            with dve.Fori(1, CHUNKS // 4) as i:
                for h in range(2):
                    step(2 * i + h, h, True)
            add_pair(CHUNKS // 2 - 1)
            dve.wait_ge(y_added, PAIR * CHUNKS // 2 + 4)
            for k in range(KD):
                dve.wait_ge(x1_in, 16 * (k + 1))
                nc.vector.scalar_tensor_tensor(out=y[:, k], in0=y[:, k], scalar=keep.mod[:, 5 * KD + k:5 * KD + k + 1], in1=v_raw[:, k % 2],
                                               op0=ALU.mult, op1=ALU.add).then_inc(out_done, 1)

        @block.tensor
        def _(pe):
            def activations(p):
                for s in range(2):
                    c = 2 * p + s
                    pe.wait_ge(u_lo_done, c + 3)
                    pe.wait_ge(act_done, c + 1)
                    for k in range(KD):
                        for c0, c1 in split_columns(T):
                            last = product3(nc, ps_a[:, s, c0:c1], u_hi[:, s, k], u_lo[:, s, k], keep.h2_hi[:, k, c0:c1], keep.h2_lo[:, k, c0:c1],
                                            k == 0, k == KD - 1)
                    last.then_inc(a_ready, 1)

            def outputs(p, h):
                pe.wait_ge(wa_lo_done, 2 * p + 4)
                pe.wait_ge(v_lo_done, 2 * p + 4)
                for j in range(PIECES):
                    d, c0 = j // 2, (j % 2) * HALF
                    pe.wait_ge(y_added, PAIR * p + (j + 1))
                    for s in range(2):
                        r = 2 * h + s
                        last = product3(nc, ps_y[:, j % 4], v_hi[:, r, d * P:(d + 1) * P], v_lo[:, r, d * P:(d + 1) * P],
                                        wa_hi[:, r, c0:c0 + HALF], wa_lo[:, r, c0:c0 + HALF], s == 0, s == 1)
                    last.then_inc(y_ready, 1)

            pe.sem_inc(a_ready, 2)
            pe.sem_inc(y_ready, 2 * PAIR)
            activations(0)
            activations(1)
            outputs(0, 0)
            with pe.Fori(1, CHUNKS // 4) as i:
                for h in range(2):
                    activations(2 * i + h)
                    outputs(2 * i + h - 1, 1 - h)
            outputs(CHUNKS // 2 - 1, 1)


class Keep:
    pass


def build(nc, io, upto=99):
    with ExitStack() as ctx:
        keep = Keep()
        m = Pool(nc, ctx, "keep")
        keep.norm_w = m.sb("norm_w", [P, 2 * KD])
        keep.mod = m.sb("mod", [P, 6 * KD])
        keep.mod_c = m.sb("mod_c", [P, 2 * KD])
        keep.gain = m.sb("gain", [P, 3, KD])
        with ExitStack() as front:
            f = Pool(nc, front, "front")
            context = front.enter_context(ExitStack())
            fc = Pool(nc, context, "front_ctx")
            lat = [f.sb(x, [P, KD, T], F32R) for x in ("h_hi", "h_lo")]
            con = [fc.sb(x, [P, KD, C], F32R) for x in ("h_hi", "h_lo")]
            keep.h_hi, keep.h_lo = Columns(lat[0], con[0]), Columns(lat[1], con[1])
            adaln_and_norm1(nc, io, keep)
            if upto < 1:
                return
            for name, shape in (("v", (TC, HEADS * HD)), ("oa", (PAIRS, P, T)), ("ob", (BLOCKS, P, T)), ("mg", (KD, P, T)), ("x1", (KD, P, T)),
                                ("gm", (NK, P, T))):
                io[name + "_scr"] = nc.dram_tensor(name + "_scratch", shape, F32, kind="Internal").ap()
            values(nc, io, keep)
            attention(nc, io, keep)
            if upto < 2:
                return
            recurrence(nc, io, keep)
            context.close()
            if upto < 3:
                return
            merge(nc, io, keep)
        b = Pool(nc, ctx, "back")
        keep.h2_hi = b.sb("h2_hi", [P, KD, T], F32R)
        keep.h2_lo = b.sb("h2_lo", [P, KD, T], F32R)
        project(nc, io, keep)
        if upto < 4:
            return
        with ExitStack() as chosen:
            c = Pool(nc, chosen, "chosen")
            keep.best = c.sb("best", [P, TT, 2 * PH, TOPK])
            keep.place = c.sb("place", [P, TT, 2 * PH, TOPK])
            route(nc, io, keep)
            if upto < 5:
                return
            gates(nc, io, keep)
        if upto < 6:
            return
        experts(nc, io, keep)


IN_SHAPES = {
    "xt": (P, KD * T), "ctxt": (P, KD * C), "cc": (P, KD * 2), "w_ada": (24, P, KD * 256), "b_ada": (P, 6 * KD),
    "norm_w": (P, 2 * KD), "w_v": (P, KD * 512), "w_q": (PAIRS, P, KD * P), "w_k": (PAIRS, P, KD * P), "qk_w": (P, 2), "mask": (P, GRID_W),
    "ident": (P, P), "head_ones": (P, P), "rpb": (PAIRS, P, DR * GRID_W),
    "w_xr": (BLOCKS + 1, P, KD * P), "w_yr": (BLOCKS + 1, P, KD * P), "lru_vec": (P, BLOCKS * NVEC), "w_gates": (BLOCKS, P, 4 * P),
    "w_ga": (KD + 1, P, KD * P), "w_gb": (KD + 1, P, KD * P), "w_oa": (KD, P, PAIRS * P), "w_ol": (KD, P, KD * P), "w_out": (KD + 2, P, KD * P),
    "w_pq": (2 * PH + 1, P, KD * P), "keys": (P, 2 * PH * NK), "iota": (P, NK), "u": (NK + 2, P, KD * P), "v": (NK, P, D),
}


def by_partition(v):
    return np.ascontiguousarray(v.reshape(-1, P).T)


def chunks(w, n):
    k, cols = w.shape
    return np.ascontiguousarray(w.reshape(k // P, P, cols // n, n).transpose(2, 1, 0, 3)).reshape(cols // n, P, -1)


def layout(inp):
    a = {k: np.asarray(v) for k, v in inp.items()}
    out = {}
    rows = lambda v: np.ascontiguousarray(v.T.reshape(KD, P, -1).transpose(1, 0, 2)).reshape(P, -1)
    out["xt"] = rows(a["x"][0])
    out["ctxt"] = rows(a["ctx"][0])
    out["cc"] = rows(np.concatenate([a["c"], a["c_ctx"][None]], axis=0))
    out["w_ada"] = chunks(a["w_ada"][0], 256)
    out["b_ada"] = by_partition(a["b_ada"][0])
    out["norm_w"] = by_partition(np.concatenate([a["norm1_w"][0], a["norm2_w"][0]]))
    w_in = a["w_in"][0]
    na = HEADS * HD
    out["w_q"] = chunks(w_in[:, 0:na], P)
    out["w_k"] = chunks(w_in[:, na:2 * na], P)
    out["w_v"] = chunks(w_in[:, 2 * na:3 * na], na)[0]
    out["qk_w"] = np.stack([np.tile(a["q_norm_w"][0], 2), np.tile(a["k_norm_w"][0], 2)], axis=1)
    xr0 = 3 * na
    again = lambda w, n=1: np.concatenate([w, w[:n]])
    out["w_xr"] = again(chunks(w_in[:, xr0:xr0 + D], P))
    out["w_yr"] = again(chunks(w_in[:, xr0 + D:xr0 + 2 * D], P))
    out["w_ga"] = again(chunks(w_in[:, xr0 + 2 * D:xr0 + 3 * D], P))
    out["w_gb"] = again(chunks(w_in[:, xr0 + 3 * D:], P))
    out["w_oa"], out["w_ol"] = (chunks(a[n][0], P) for n in ("w_o_attn", "w_o_lru"))
    out["w_out"] = again(chunks(a["w_out"][0], P), 2)
    out["w_pq"] = again(chunks(a["peer_w_q"][0], P))
    out["keys"] = np.ascontiguousarray(a["peer_keys"][0].transpose(3, 0, 1, 2)).reshape(P, -1)
    out["iota"] = np.tile(np.arange(NK, dtype=np.float32), (P, 1))
    u = a["peer_u"][0].reshape(NK, NK, KD, P).transpose(0, 3, 2, 1).reshape(NK, P, KD * P)
    out["u"] = np.concatenate([u, u[:2]])
    out["v"] = a["peer_v"][0].reshape(NK, NK, D)
    bias4 = np.stack([a["lru_b_a"][0, 0], a["lru_b_x"][0, 0], a["lru_b_a"][0, 1], a["lru_b_x"][0, 1]])
    vec = np.concatenate([a["conv_w"][0], a["conv_b"], bias4, a["lru_lambda"][0]])
    out["lru_vec"] = np.ascontiguousarray(vec.reshape(NVEC, BLOCKS, P).transpose(2, 1, 0)).reshape(P, -1)
    gates = np.stack([a["lru_w_a"][0, 0], a["lru_w_x"][0, 0], a["lru_w_a"][0, 1], a["lru_w_x"][0, 1]], axis=2)
    out["w_gates"] = gates.reshape(BLOCKS, P, 4 * P)
    rpb = a["na_rpb"][0]
    mask = np.full((GRID_W, GRID_W), NEG, np.float32)
    bias = np.zeros((HEADS, GRID_W, DR, GRID_W), np.float32)
    for c in range(GRID_W):
        lo = min(max(c - WIN_COLS // 2, 0), GRID_W - WIN_COLS)
        mask[c, lo:lo + WIN_COLS] = 0.0
        first = lo - c + WIN_COLS - 1
        bias[:, c, :, lo:lo + WIN_COLS] = rpb[:, :, first:first + WIN_COLS]
    out["mask"] = np.tile(mask, (2, 1))
    out["rpb"] = bias.reshape(PAIRS, P, DR * GRID_W)
    out["ident"] = np.eye(P, dtype=np.float32)
    out["head_ones"] = np.kron(np.eye(2, dtype=np.float32), np.ones((HD, HD), np.float32))
    return out


def kernel(**inputs):
    import concourse.bacc as bacc
    from concourse.bass_utils import run_bass_kernel_spmd

    arrays = layout(inputs)
    nc = bacc.Bacc("TRN2", target_bir_lowering=False, num_devices=1)
    io = {name: nc.dram_tensor("in_" + name, shape, F32, kind="ExternalInput").ap() for name, shape in IN_SHAPES.items()}
    io["out"] = nc.dram_tensor("out", (P, KD * T), F32, kind="ExternalOutput").ap()
    build(nc, io)
    r = run_bass_kernel_spmd(nc, [{"in_" + name: arrays[name] for name in IN_SHAPES}], core_ids=[0])
    y = np.asarray(r.results[0]["out"]).reshape(P, KD, T)
    return np.ascontiguousarray(y.transpose(2, 1, 0)).reshape(1, T, D)
```
